# Optimizing a Trainium2 kernel written in Bass

```python
import math
import jax, jax.numpy as jnp
from jax import lax
import numpy as np

D_MODEL = 1024
BATCH = 1
SEQ = 1024
DEPTH = 1

ATTN_HEADS = 8
ATTN_HEAD_DIM = 64
ATTN_V_DIM = 2 * ATTN_HEAD_DIM
ATTN_WIDTH = ATTN_HEADS * 2 * ATTN_HEAD_DIM
Q_BLOCK = 128
CONV_WIDTH = 512
CONV_K = 3
POOL_WINDOWS = (2, 4, 8, 16)
POOL_GROUP = 128
POOL_WIDTH = POOL_GROUP * len(POOL_WINDOWS)
N_BRANCH = 3
D_FF = -(-8 * D_MODEL // (3 * 256)) * 256
EPS = 1e-6

OFF_Q = 0
OFF_K = OFF_Q + ATTN_WIDTH
OFF_V = OFF_K + ATTN_WIDTH
OFF_CB = OFF_V + ATTN_WIDTH
OFF_CC = OFF_CB + CONV_WIDTH
OFF_CH = OFF_CC + CONV_WIDTH
OFF_POOL = OFF_CH + CONV_WIDTH
OFF_GATE = OFF_POOL + POOL_WIDTH
IN_COLS = OFF_GATE + N_BRANCH * D_MODEL

kernel_name = "hybrid_diffattn_conv_pool_gated"

def rms_norm(x, g):
    xf = x.astype(jnp.float32)
    y = xf * lax.rsqrt(jnp.mean(xf * xf, axis=-1, keepdims=True) + EPS)
    return (y * g.astype(jnp.float32)).astype(x.dtype)

def diff_attention(q, k, v, lam, subln_g, lambda_init):
    b, s = q.shape[0], q.shape[1]
    nb = s // Q_BLOCK
    scale = ATTN_HEAD_DIM ** -0.5
    qb = (q * scale).reshape(b, nb, Q_BLOCK, ATTN_HEADS, 2, ATTN_HEAD_DIM)
    qb = qb.transpose(1, 0, 3, 4, 2, 5)
    kt = k.transpose(0, 2, 3, 1, 4)
    vt = v.transpose(0, 2, 1, 3)
    k_pos = jnp.arange(s)

    def block(args):
        q_blk, i = args
        q_pos = i * Q_BLOCK + jnp.arange(Q_BLOCK)
        sc = jnp.einsum('bhcqd,bhckd->bhcqk', q_blk, kt).astype(jnp.float32)
        causal = k_pos[None, :] <= q_pos[:, None]
        sc = jnp.where(causal, sc, -jnp.inf)
        p = jax.nn.softmax(sc, axis=-1)
        p_diff = p[:, :, 0] - lam * p[:, :, 1]
        return jnp.einsum('bhqk,bhkv->bhqv', p_diff.astype(vt.dtype), vt)

    o = lax.map(block, (qb, jnp.arange(nb)))
    o = rms_norm(o, subln_g) * (1.0 - lambda_init)
    return o.transpose(1, 0, 3, 2, 4).reshape(b, s, ATTN_HEADS * ATTN_V_DIM)

def short_conv(u, w):
    s = u.shape[1]
    up = jnp.pad(u, ((0, 0), (CONV_K - 1, 0), (0, 0)))
    return sum(up[:, j:j + s] * w[j] for j in range(CONV_K))

def multiscale_pool(u, pool_w, pool_scale):
    s = u.shape[1]
    uf = u.astype(jnp.float32)
    cs = jnp.cumsum(uf, axis=1)
    t = jnp.arange(1, s + 1, dtype=jnp.float32)[None, :, None]
    outs = []
    for gi, w in enumerate(POOL_WINDOWS):
        sl = slice(gi * POOL_GROUP, (gi + 1) * POOL_GROUP)
        cg = cs[..., sl]
        prev = jnp.pad(cg, ((0, 0), (w, 0), (0, 0)))[:, :s]
        mean = (cg - prev) / jnp.minimum(t, float(w))
        d = (mean - uf[..., sl]).astype(u.dtype)
        outs.append(jnp.einsum('bsc,cd->bsd', d, pool_w[gi]))
    return jnp.concatenate(outs, axis=-1) * pool_scale

def setup_inputs(seed: int = 0) -> dict:
    key = jax.random.key(seed)
    ks = jax.random.split(key, 24)
    f32 = jnp.float32
    nrm = lambda k, shape, fan_in: jax.random.normal(k, shape, f32) * fan_in ** -0.5
    gain = lambda k, shape: 1.0 + 0.02 * jax.random.normal(k, shape, f32)
    L, D = DEPTH, D_MODEL
    return {
        "x": jax.random.normal(ks[0], (BATCH, SEQ, D), f32),
        "g_pre_mix": gain(ks[1], (L, D)),
        "w_in": nrm(ks[2], (L, D, IN_COLS), D),
        "b_gate": 0.02 * jax.random.normal(ks[3], (L, N_BRANCH * D), f32),
        "lambda_q1": 0.1 * jax.random.normal(ks[4], (L, ATTN_HEAD_DIM), f32),
        "lambda_k1": 0.1 * jax.random.normal(ks[5], (L, ATTN_HEAD_DIM), f32),
        "lambda_q2": 0.1 * jax.random.normal(ks[6], (L, ATTN_HEAD_DIM), f32),
        "lambda_k2": 0.1 * jax.random.normal(ks[7], (L, ATTN_HEAD_DIM), f32),
        "subln_g": gain(ks[8], (L, ATTN_V_DIM)),
        "w_attn_proj": nrm(ks[9], (L, ATTN_WIDTH, D), ATTN_WIDTH),
        "conv_w": nrm(ks[10], (L, CONV_K, CONV_WIDTH), CONV_K),
        "w_conv_proj": nrm(ks[11], (L, CONV_WIDTH, D), CONV_WIDTH),
        "pool_w": nrm(ks[12], (L, len(POOL_WINDOWS), POOL_GROUP, POOL_GROUP), POOL_GROUP),
        "pool_scale": 1.0 + 0.1 * jax.random.normal(ks[13], (L, POOL_WIDTH), f32),
        "w_pool_proj": nrm(ks[14], (L, POOL_WIDTH, D), POOL_WIDTH),
        "w_out": nrm(ks[15], (L, D, D), D),
        "g_post_mix": gain(ks[16], (L, D)),
        "g_pre_ffn": gain(ks[17], (L, D)),
        "w_gate_up": nrm(ks[18], (L, D, 2 * D_FF), D),
        "w_down": nrm(ks[19], (L, D_FF, D), D_FF),
        "g_post_ffn": gain(ks[20], (L, D)),
    }

def reference(x, g_pre_mix, w_in, b_gate, lambda_q1, lambda_k1, lambda_q2, lambda_k2,
              subln_g, w_attn_proj, conv_w, w_conv_proj, pool_w, pool_scale, w_pool_proj,
              w_out, g_post_mix, g_pre_ffn, w_gate_up, w_down, g_post_ffn):
    b, s, d = x.shape
    for l in range(DEPTH):
        xn = rms_norm(x, g_pre_mix[l])
        z = jnp.einsum('bsd,dc->bsc', xn, w_in[l])

        q = z[..., OFF_Q:OFF_K].reshape(b, s, ATTN_HEADS, 2, ATTN_HEAD_DIM)
        k = z[..., OFF_K:OFF_V].reshape(b, s, ATTN_HEADS, 2, ATTN_HEAD_DIM)
        v = z[..., OFF_V:OFF_CB].reshape(b, s, ATTN_HEADS, ATTN_V_DIM)
        lambda_init = 0.8 - 0.6 * math.exp(-0.3 * l)
        lam = (jnp.exp(jnp.sum(lambda_q1[l].astype(jnp.float32) * lambda_k1[l].astype(jnp.float32)))
               - jnp.exp(jnp.sum(lambda_q2[l].astype(jnp.float32) * lambda_k2[l].astype(jnp.float32)))
               + lambda_init)
        y_attn = diff_attention(q, k, v, lam, subln_g[l], lambda_init)

        gb = z[..., OFF_CB:OFF_CC]
        gc = z[..., OFF_CC:OFF_CH]
        hc = z[..., OFF_CH:OFF_POOL]
        y_conv = gb * short_conv(gc * hc, conv_w[l])

        y_pool = multiscale_pool(z[..., OFF_POOL:OFF_GATE], pool_w[l], pool_scale[l])

        gates = jax.nn.sigmoid(z[..., OFF_GATE:] + b_gate[l]).reshape(b, s, N_BRANCH, d)
        merged = (gates[:, :, 0] * jnp.einsum('bsc,cd->bsd', y_attn, w_attn_proj[l])
                  + gates[:, :, 1] * jnp.einsum('bsc,cd->bsd', y_conv, w_conv_proj[l])
                  + gates[:, :, 2] * jnp.einsum('bsc,cd->bsd', y_pool, w_pool_proj[l]))
        mix = jnp.einsum('bsd,de->bse', merged, w_out[l])
        x = x + rms_norm(mix, g_post_mix[l])

        hn = rms_norm(x, g_pre_ffn[l])
        gu = jnp.einsum('bsd,df->bsf', hn, w_gate_up[l])
        hf = jax.nn.silu(gu[..., :D_FF]) * gu[..., D_FF:]
        ff = jnp.einsum('bsf,fd->bsd', hf, w_down[l])
        x = x + rms_norm(ff, g_post_ffn[l])
    return x


_drawn_inputs = setup_inputs


def setup_inputs(seed=0):
    import zlib

    import numpy as np

    out = dict(_drawn_inputs(seed))
    spreads = {}
    factors = {'b_gate': 8.0,
     'lambda_k1': 4.161,
     'lambda_q2': 4.429,
     'subln_g': 6.254,
     'g_post_mix': 3.472,
     'g_pre_ffn': 3.462,
     'g_post_ffn': 18.538,
     'pool_scale': 2.692}
    for name, (base, spread) in spreads.items():
        noise = np.random.default_rng([zlib.crc32(name.encode()), seed]).standard_normal(out[name].shape)
        drawn = base * np.exp(spread * noise) if base else spread * noise
        out[name] = __import__('jax').numpy.asarray(drawn.astype(out[name].dtype))
    for name, factor in factors.items():
        out[name] = (out[name] * factor).astype(out[name].dtype)
    return out
```

```python
import math
from contextlib import ExitStack, contextmanager

import concourse.bass as bass
from concourse import mybir

F32 = mybir.dt.float32
F32R = mybir.dt.float32r
BF16 = mybir.dt.bfloat16
ALU = mybir.AluOpType
ACT = mybir.ActivationFunctionType
AX_X = mybir.AxisListType.X

P = 128
HALF = 512
EPS = 1e-6
MASKED = -1e30
WINDOWS = (2, 4, 8, 16)
HH, LL = 0, 1
PASSES = ((HH, HH), (HH, LL), (LL, HH))


class Count:

    def __init__(self):
        self.first, self.step, self.turn = 0, 0, 0

    def at(self, plus=0):
        v = self.first + plus
        return self.turn * self.step + v if self.step else v

    def slot(self, ring, plus=0):
        assert self.step % ring == 0
        return (self.first + plus) % ring

    def rounds(self, ring, plus=0):
        v = (self.first + plus) // ring
        return self.turn * (self.step // ring) + v if self.step else v

    def next(self, by=1):
        self.first += by


@contextmanager
def turns(eng, n, advance):
    before = {c: c.first for c in advance}
    with eng.Fori(0, n) as turn:
        for c, step in advance.items():
            c.step, c.turn = step, turn
        yield turn
        for c, step in advance.items():
            assert c.first - before[c] == step, (c.first - before[c], step)
            c.first, c.step, c.turn = before[c] + n * step, 0, 0


def wait_for(eng, sem, value):
    if not isinstance(value, int) or value > 0:
        eng.wait_ge(sem, value)


def wait_apart(eng, passed, sem, value):
    wait_for(eng, sem, value)
    if not isinstance(value, int):
        eng.sem_inc(passed, 1)


def build(nc, x, g_pre_mix, w_in, b_gate, lambda_q1, lambda_k1, lambda_q2, lambda_k2, subln_g,
          w_attn_proj, conv_w, w_conv_proj, pool_w, pool_scale, w_pool_proj, w_out, g_post_mix,
          g_pre_ffn, w_gate_up, w_down, g_post_ffn, out):
    _, S, D = x.shape
    HD = lambda_q1.shape[1]
    HV = 2 * HD
    HEADS = w_attn_proj.shape[1] // HV
    CW = conv_w.shape[2]
    CT = CW // P
    KT = D // P
    TT = S // P
    FF = w_down.shape[1]
    FT = FF // P
    FC = FT // 2
    LAMBDA_INIT = 0.8 - 0.6 * math.exp(-0.3 * 0)
    assert S == D == 2 * HALF and KT == TT == HEADS == 8 and HV == P and CT == len(WINDOWS) == 4 and FC == 11
    OFF_Q, OFF_K, OFF_V = 0, D, 2 * D
    OFF_CB = 3 * D
    OFF_CC, OFF_CH, OFF_POOL = OFF_CB + CW, OFF_CB + 2 * CW, OFF_CB + 3 * CW
    OFF_GATE = OFF_POOL + len(WINDOWS) * P
    GROUPS = 2 * TT + 4 * KT + 4 * 4 + 6 * CT + 4 * KT + 4 * KT + 2 * TT + 8 * FC + 2 * TT * (FC - 1)

    ctx = ExitStack()
    with ctx:
        def sem(name):
            return ctx.enter_context(nc.semaphore(name))

        BASE = 16512
        R1 = BASE
        R2 = R1 + 65536
        R2B = R2 + 32768
        RF = R2 + 65536
        RRAW = RF + 32768
        RRING = RRAW + 8192
        RT = RRING + 16384
        RM = RT + 4096
        RC = RM + 4 * 4096 + 32
        consts_at = [RC]

        def at(name, shape, dt, offset):
            return nc.alloc_sbuf_tensor_at(name, shape, dt, offset=offset)

        def const(name, shape, dt=F32):
            size = math.prod(shape[1:]) * (2 if dt == BF16 else 4)
            t = at(name, shape, dt, consts_at[0])
            consts_at[0] += (size + 31) // 32 * 32
            return t

        xn = at("xn", [P, 2, KT, S], F32R, R1)
        w_o = at("w_o", [P, 2, KT, D], F32R, R1)
        ff_sum = at("ff_sum", [P, TT, D], F32, R1)
        hf = at("hf", [P, 2, 2, 2, S], F32R, R1 + 32768)

        w_v = at("w_v", [P, 2, KT, D], F32R, R2)
        qt = at("qt", [P, 2, 2, S], F32R, R2)
        kt = at("kt", [P, 2, 2, S], F32R, R2 + 16384)
        vh = at("vh", [P, 2, 2, TT, HV], F32R, R2 + 32768)
        pt = at("pt", [P, 2, 2, TT, P], F32R, R2 + 49152)
        ya = at("ya", [P, 2, HEADS, S], F32R, R2)
        u_pad = at("u_pad", [P, 16 + S], F32, R2)
        sum_a = at("sum_a", [P, 16 + S], F32, R2 + 4160)
        sum_b = at("sum_b", [P, 16 + S], F32, R2 + 8320)
        d_raw = at("d_raw", [P, S], F32, R2 + 12480)
        dh = at("dh", [P, 2, S], F32R, R2 + 16576)
        w_pool = at("w_pool", [P, 2, 4, P], F32R, R2 + 24768)
        yc = at("yc", [P, 2, CT, S], F32R, R2)
        gate_c = at("gate_c", [P, KT, S], F32, R2)
        yp = at("yp", [P, 2, CT, S], F32R, R2B)
        hn = at("hn", [P, 2, KT, S], F32R, R2)

        x_tile = at("x_tile", [P, 2, D], F32, RF)
        xs_tile = at("xs_tile", [P, 2, D], F32, RF + 8192)
        g_pre_mix_b = at("g_pre_mix_b", [P, D], F32, RF + 16384)
        v_out = at("v_out", [P, 2, 2, HALF], F32, RF + 20480)
        e_t = at("e_t", [P, 2, 2, S], F32, RF)
        diff = at("diff", [P, 2, S], F32, RF + 16384)
        v_raw = at("v_raw", [P, TT, HV], F32, RF + 24576)
        y_row = at("y_row", [P, 2, HV], F32, RF + 28672)
        junk_o = at("junk_o", [P, HV], F32, RF + 28672 + 1024)
        u_lo = at("u_lo", [P, HV], F32, RF + 28672 + 1536)
        u_row = at("u_row", [P, 2, HV], F32, RF + 28672 + 2048)
        merged = at("merged", [P, KT, S], F32, RF)
        w_d = at("w_d", [P, 2, 2, 2, D], F32R, RF)

        raw_first = at("raw_first", [P, KT // 2, 1024], F32, RM)
        raw = at("raw", [P, 2, 1024], F32, RRAW)
        ring = at("ring", [P, 2, 2, 1024], F32R, RRING)

        y_out = at("y_out", [P, 2, 2, S], F32R, RM)
        gate = at("gate", [P, 2, S], F32, RM)
        gated = at("gated", [P, 2, HALF], F32, RM + 8192)
        conv_c = at("conv_c", [P, S], F32, RM)
        conv_in = at("conv_in", [P, 2 + S], F32, RM + 4096)
        conv_sum = at("conv_sum", [P, S], F32, RM + 8224)
        y_raw = at("y_raw", [P, S], F32, RM + 12320)
        g_post_mix_b = at("g_post_mix_b", [P, D], F32, RM)
        g_pre_ffn_b = at("g_pre_ffn_b", [P, D], F32, RM + 4096)
        x1 = at("x1", [P, 2, D], F32, RM + 8192)
        row = at("row", [P, D], F32, RT)
        silu = at("silu", [P, S], F32, RM)
        hf_raw = at("hf_raw", [P, S], F32, RM + 4096)
        g_post_ffn_b = at("g_post_ffn_b", [P, D], F32, RM)
        x1_again = at("x1_again", [P, TT, D], F32, R2)
        out_t = at("out_t", [P, TT, D], F32, R2B)

        ident = const("ident", [P, P])
        select = const("select", [P, 2, P], BF16)
        mask = const("mask", [P, 2, P], BF16)
        bias_g = const("bias_g", [P, 3 * KT])
        conv_k = const("conv_k", [P, 3, CT])
        scale_p = const("scale_p", [P, CT])
        over_t = const("over_t", [P, 16])
        first_w = const("first_w", [P, 16])
        g_sub = const("g_sub", [P, HV])
        minus_half = const("minus_half", [P, 1])
        ssq = const("ssq", [P, 2, 4])
        rstd = const("rstd", [P, 2, 4])
        lam_in = const("lam_in", [P, 4, HD])
        lam_dot = const("lam_dot", [P, 2])
        lam_exp = const("lam_exp", [P, 2])
        neg_lam = const("neg_lam", [P, 1])
        neg_max = const("neg_max", [P, 2, 2])
        sums = const("sums", [P, 4, 2])
        rsums = const("rsums", [P, 4, 2])
        d_scale = const("d_scale", [P, 2])
        o_ssq = const("o_ssq", [P, 2])
        o_scale = const("o_scale", [P, 2])
        assert consts_at[0] <= 229344, consts_at[0]

        ps = ctx.enter_context(nc.psum_tensor("ps", [P, 8, 512], F32))
        TB = (4, 5)
        U_BANK, PROJ_BANK = 6, 7

        v_dram = nc.dram_tensor("v_scratch", (S, D), F32).ap()
        y_dram = nc.dram_tensor("y_scratch", (HEADS, P, 2 * S), F32).ap()
        x1_dram = nc.dram_tensor("x1_scratch", (S, D), F32).ap()

        raw_landed = [sem(f"raw_landed{i}") for i in range(2)]
        first_landed = [sem(f"first_landed{i}") for i in range(KT // 2)]
        w_hi, w_lo = sem("w_hi"), sem("w_lo")
        groups_done = sem("groups_done")
        evacuated = [sem(f"evacuated{i}") for i in range(4)]
        tr_done = [sem(f"tr_done{i}") for i in range(2)]
        tr_free = [sem(f"tr_free{i}") for i in range(2)]
        tr_hi = sem("tr_hi")
        ident_ready, half_ready, mask_ready = sem("ident_ready"), sem("half_ready"), sem("mask_ready")
        small_landed, lam_landed, over_ready = sem("small_landed"), sem("lam_landed"), sem("over_ready")
        g1_landed, g2_landed, g3_landed = sem("g1_landed"), sem("g2_landed"), sem("g3_landed")
        x_first = [sem(f"x_first{i}") for i in range(2)]
        x_landed = [sem(f"x_landed{i}") for i in range(2)]
        squared, rstd_ready, rows_ready = sem("squared"), sem("rstd_ready"), sem("rows_ready")
        sp_passed, act_passed, pool_passed = sem("sp_passed"), sem("act_passed"), sem("pool_passed")
        pool_step, dve_step = sem("pool_step"), sem("dve_step")
        v_stored = [sem(f"v_stored{i}") for i in range(4)]
        lam_dots, lam_exps = sem("lam_dots"), sem("lam_exps")
        v_landed, v_hi, v_lo = sem("v_landed"), sem("v_hi"), sem("v_lo")
        proj_done, proj_hi, proj_lo = sem("proj_done"), sem("proj_hi"), sem("proj_lo")
        scores_done, max_ready, exp_done = sem("scores_done"), sem("max_ready"), sem("exp_done")
        diff_ready = sem("diff_ready")
        u_lo_ready, u_ready = sem("u_lo_ready"), sem("u_ready")
        pv_done, o_squared, o_scaled, y_ready = sem("pv_done"), sem("o_squared"), sem("o_scaled"), sem("y_ready")
        y_stored = [sem(f"y_stored{i}") for i in range(2)]
        y_free, y_landed = sem("y_free"), sem("y_landed")
        pads_ready = sem("pads_ready")
        d_ready, d_hi, d_lo = sem("d_ready"), sem("d_hi"), sem("d_lo")
        yp_hi, yc_hi, yc_lo = sem("yp_hi"), sem("yc_hi"), sem("yc_lo")
        merged_ready = sem("merged_ready")
        m_hi, m_lo = sem("m_hi"), sem("m_lo")
        x1_ready, x1_squared, hn_rows = sem("x1_ready"), sem("x1_squared"), sem("hn_rows")
        x1_stored = [sem(f"x1_stored{i}") for i in range(2)]
        hf_hi, hf_lo = sem("hf_hi"), sem("hf_lo")
        sum_zero = sem("sum_zero")
        out_ready = sem("out_ready")
        out_stored = sem("out_stored")
        x1_landed = sem("x1_landed")

        def wait_evacuated(eng, g, plus=0):
            eng.wait_ge(evacuated[g.slot(4, plus)], g.rounds(4, plus + 4))

        block = ctx.enter_context(nc.Block())

        @block.sync
        def _(sp):
            n = Count()

            def load(src, cols=P, early=False):
                slot = n.slot(2)
                if not early:
                    wait_apart(sp, sp_passed, w_lo, n.at(-1))
                dst = raw[:, slot, :]
                if cols:
                    dst = dst.rearrange("p (k c) -> p k c", c=cols)[:, 0:src.shape[1], :]
                sp.dma_start(dst, src).then_inc(raw_landed[slot], 16)
                n.next()

            def tile_of(w, first, cols=P):
                return w[0].rearrange("(k p) c -> p k c", p=P)[:, :, bass.ds(first, cols)]

            for m in range(KT // 2):
                sp.dma_start(raw_first[:, m, :].rearrange("p (k c) -> p k c", c=P), tile_of(w_in, OFF_V + P * m))\
                    .then_inc(first_landed[m], 16)
            n.next(KT // 2)
            for m in range(KT // 2, KT):
                load(tile_of(w_in, OFF_V + P * m), early=m < KT // 2 + 2)
            for h in range(2):
                load(tile_of(w_in, OFF_K + P * h))
                load(tile_of(w_in, OFF_Q + P * h))
            with turns(sp, (HEADS - 2) // 2, {n: 4}) as it:
                for j in range(2):
                    load(tile_of(w_in, it * (2 * P) + (OFF_K + P * (2 + j))))
                    load(tile_of(w_in, it * (2 * P) + (OFF_Q + P * (2 + j))))
            with turns(sp, KT // 2, {n: 2}) as it:
                for j in range(2):
                    load(tile_of(w_in, it * (2 * P) + (OFF_GATE + P * j)))
            with turns(sp, KT // 2, {n: 2}) as it:
                for j in range(2):
                    load(tile_of(w_attn_proj, it * (2 * P) + P * j))
            for c in range(4):
                load(tile_of(w_in, OFF_POOL + P * c))
                if c == 0:
                    load(pool_w[0].rearrange("g c d -> c g d"))
            for c in range(CT):
                for off in (OFF_CC, OFF_CH, OFF_CB):
                    load(tile_of(w_in, off + P * c))
            with turns(sp, KT // 4, {n: 6}) as it:
                for j in range(2):
                    for i in range(2):
                        load(tile_of(w_in, it * (4 * P) + (OFF_GATE + D + P * (2 * j + i))))
                    load(tile_of(w_conv_proj, it * (4 * P) + 2 * P * j, 2 * P), 2 * P)
            with turns(sp, KT // 2, {n: 2}) as it:
                for j in range(2):
                    load(tile_of(w_in, it * (2 * P) + (OFF_GATE + 2 * D + P * j)))
            for m2 in range(KT // 2):
                load(tile_of(w_pool_proj, 2 * P * m2, 2 * P), 2 * P)
                for i in range(2):
                    load(tile_of(w_out, P * (2 * m2 + i)))

            def ffn_chunk(c):
                for f in range(2):
                    load(tile_of(w_gate_up, c * (2 * P) + P * f))
                    load(tile_of(w_gate_up, c * (2 * P) + (P * f + FF)))
                for f in range(2):
                    load(w_down[0, bass.ds(c * (2 * P) + P * f, P), :], 0)

            ffn_chunk(0)
            with turns(sp, (FC - 3) // 2, {n: 12}) as it:
                ffn_chunk(it * 2 + 1)
                ffn_chunk(it * 2 + 2)
            ffn_chunk(FC - 2)
            ffn_chunk(FC - 1)
            for i in range(TT):
                sp.wait_ge(out_ready, i + 1)
                sp.dma_start(out[0, P * i:P * (i + 1), :], out_t[:, i, :]).then_inc(out_stored, 16)
            sp.wait_ge(out_stored, 16 * TT)

        @block.gpsimd
        def _(pool):
            x_h = x[0]
            step, g = Count(), Count()

            def did(ins):
                ins.then_inc(pool_step, 1)
                step.next()
                pool.wait_ge(pool_step, step.at())

            def rstd_of(b, kind):
                pool.wait_ge(half_ready, 1)
                did(pool.tensor_scalar(rstd[:, b, kind:kind + 1], ssq[:, b, kind:kind + 1], 1.0 / D, EPS,
                                       ALU.mult, ALU.add))
                pool.tensor_tensor(rstd[:, b, kind:kind + 1], rstd[:, b, kind:kind + 1], minus_half[:, :],
                                   ALU.pow).then_inc(rstd_ready, 1)

            did(pool.memset(ident[:, :], 0.0))
            pool.affine_select(out=ident[:, :], in_=ident[:, :], compare_op=ALU.not_equal, fill=1.0,
                               base=0, pattern=[[-1, P]], channel_multiplier=1).then_inc(ident_ready, 1)
            pool.memset(minus_half[:, :], -0.5).then_inc(half_ready, 1)

            def store_v(i):
                for half in range(2):
                    wait_evacuated(pool, g)
                    pool.dma_start(v_dram[P * i:P * (i + 1), HALF * half:HALF * (half + 1)], v_out[:, i % 2, half, :])\
                        .then_inc(v_stored[2 * (i % 2) + half], 16)
                    g.next()

            for i in range(TT):
                pool.wait_ge(squared, i + 1)
                wait_for(pool, rows_ready, i - 1)
                rstd_of(i % 2, 0)
                if i + 2 < TT:
                    pool.wait_ge(rows_ready, i + 1)
                    pool.dma_start(x_tile[:, i % 2, :], x_h[P * (i + 2):P * (i + 3), :])\
                        .then_inc(x_landed[i % 2], 16)
                if i == 0:
                    for n, lam in enumerate((lambda_q1, lambda_k1, lambda_q2, lambda_k2)):
                        pool.dma_start(lam_in[:, n, :], lam[0, :].partition_broadcast(P)).then_inc(lam_landed, 16)
                    pool.dma_start(g_sub[:, :], subln_g[0, :].partition_broadcast(P)).then_inc(lam_landed, 16)
                if i >= 2:
                    store_v(i - 2)
            for t0 in range(16):
                pool.memset(over_t[:, t0:t0 + 1], 1.0 / (t0 + 1)).then_inc(over_ready, 1)
            pool.wait_ge(over_ready, 16)
            for c in range(2):
                part = slice(64 * c, 64 * c + 64)
                for n in range(2):
                    did(pool.memset(select[part, n, :], 0.0))
                    did(pool.affine_select(out=select[part, n, :], in_=select[part, n, :],
                                           compare_op=ALU.not_equal, fill=1.0, base=64 * n,
                                           pattern=[[-1, P]], channel_multiplier=1))
                    did(pool.memset(mask[part, n, :], 0.0))
                    pool.affine_select(out=mask[part, n, :], in_=mask[part, n, :],
                                       compare_op=ALU.is_ge, fill=MASKED, base=64 * n,
                                       pattern=[[-1, P]], channel_multiplier=1).then_inc(mask_ready, 1)
                    pool.wait_ge(mask_ready, 2 * c + n + 1)
            store_v(TT - 2)
            store_v(TT - 1)
            pool.wait_ge(mask_ready, 4)

            def load_v(h):
                pool.dma_start(v_raw[:, :, :],
                               v_dram.rearrange("(t p) c -> p t c", p=P)[:, :, bass.ds(h * HV, HV)])\
                    .then_inc(v_landed, 16)

            for b in range(4):
                pool.wait_ge(v_stored[b], 16 * TT // 2)
            load_v(0)
            pool.dma_start(bias_g[:, :], b_gate[0].rearrange("(m p) -> p m", p=P),
                           allow_slow_non_contiguous=True).then_inc(small_landed, 16)
            for k in range(3):
                pool.dma_start(conv_k[:, k, :], conv_w[0, k].rearrange("(c p) -> p c", p=P),
                               allow_slow_non_contiguous=True).then_inc(small_landed, 16)
            pool.dma_start(scale_p[:, :], pool_scale[0].rearrange("(c p) -> p c", p=P),
                           allow_slow_non_contiguous=True).then_inc(small_landed, 16)

            t, heads_in, heads_out = Count(), Count(), Count()
            pool.sem_inc(y_free, 2)

            def norm(i):
                b = i % 2
                pool.wait_ge(o_squared, t.at(1))
                wait_apart(pool, pool_passed, y_ready, t.at(-1))
                did(pool.tensor_scalar(o_scale[:, b:b + 1], o_ssq[:, b:b + 1], 1.0 / HV, EPS, ALU.mult, ALU.add))
                did(pool.tensor_tensor(o_scale[:, b:b + 1], o_scale[:, b:b + 1], minus_half[:, :], ALU.pow))
                pool.tensor_tensor(o_scale[:, b:b + 1], o_scale[:, b:b + 1], rsums[:, i % 4, 0:1], ALU.mult)\
                    .then_inc(o_scaled, 1)
                t.next()

            def store_y(par, h):
                pool.wait_ge(tr_free[1], heads_out.at(1) * (TT + TT // 2) + TT)
                pool.dma_start(y_dram[bass.ds(h, 1)].rearrange("a p c -> (a p) c"),
                               y_out[:, par].rearrange("p s t -> p (s t)").bitcast(F32)).then_inc(y_stored[par], 16)
                heads_out.next()

            def head(par, h, first=False, last=False):
                if not last:
                    pool.wait_ge(v_lo, heads_in.at(1))
                    load_v(h + 1)
                    heads_in.next()
                for i in range(TT):
                    if not (first and i < 2):
                        norm((i - 2) % TT)
                    if i == 5 and not first:
                        store_y(1 - par, h - 1)
                    if i == 7 and not first:
                        pool.wait_ge(y_stored[1 - par], heads_out.rounds(2, 1) * 16)
                        pool.sem_inc(y_free, 1)

            head(0, 0, first=True)
            with turns(pool, (HEADS - 2) // 2, {t: 16, step: 32, heads_in: 2, heads_out: 2}) as it:
                head(1, it * 2 + 1)
                head(0, it * 2 + 2)
            head(1, HEADS - 1, last=True)
            norm(6)
            norm(7)
            store_y(1, HEADS - 1)
            for b in range(2):
                pool.wait_ge(y_stored[b], 16 * HEADS // 2)
            for h in range(HEADS):
                pool.dma_start(ya[:, :, h, :].bitcast(F32), y_dram[h].rearrange("p (s t) -> p s t", s=2))\
                    .then_inc(y_landed, 16)

            pool.wait_ge(groups_done, 2 * TT + 4 * KT)
            for buf in (u_pad, sum_a, sum_b):
                pool.memset(buf[:, 0:16], 0.0).then_inc(pads_ready, 1)
            pool.memset(conv_in[:, 0:2], 0.0).then_inc(pads_ready, 1)

            pool.wait_ge(merged_ready, 1)
            pool.dma_start(g_post_mix_b[:, :], g_post_mix[0, :].partition_broadcast(P)).then_inc(g2_landed, 16)
            pool.dma_start(g_pre_ffn_b[:, :], g_pre_ffn[0, :].partition_broadcast(P)).then_inc(g2_landed, 16)
            for b in range(2):
                pool.dma_start(x1[:, b, :], x_h[P * b:P * (b + 1), :]).then_inc(x_landed[b], 16)
            tile = Count()

            def residual(b, i, last=False):
                wait_apart(pool, pool_passed, squared, tile.at(TT + 1))
                rstd_of(b, 1)
                pool.wait_ge(x1_ready, tile.at(1))
                pool.dma_start(x1_dram[bass.ds(i * P, P), :], x1[:, b, :]).then_inc(x1_stored[b], 16)
                wait_apart(pool, pool_passed, x1_squared, tile.at(1))
                rstd_of(b, 2)
                if not last:
                    pool.wait_ge(x1_stored[b], tile.rounds(2, 2) * 16)
                    pool.wait_ge(hn_rows, tile.at(1))
                    pool.dma_start(x1[:, b, :], x_h[bass.ds((i + 2) * P, P), :]).then_inc(x_landed[b], 16)
                tile.next()

            with turns(pool, (TT - 2) // 2, {tile: 2, step: 4}) as it:
                residual(0, it * 2)
                residual(1, it * 2 + 1)
            residual(0, TT - 2, last=True)
            residual(1, TT - 1, last=True)

            pool.wait_ge(tr_free[0], TT + HEADS * TT + TT)
            for i in range(TT):
                pool.memset(ff_sum[:, i, :], 0.0).then_inc(sum_zero, 1)
            for b in range(2):
                pool.wait_ge(x1_stored[b], 16 * TT // 2)
            pool.wait_ge(groups_done, GROUPS - 2 * TT)
            for i in range(TT):
                pool.dma_start(x1_again[:, i, :], x1_dram[P * i:P * (i + 1), :]).then_inc(x1_landed, 16)
            pool.wait_ge(hf_lo, 2 * FT)
            pool.dma_start(g_post_ffn_b[:, :], g_post_ffn[0, :].partition_broadcast(P)).then_inc(g3_landed, 16)
            for i in range(TT):
                pool.wait_ge(squared, 2 * TT + i + 1)
                wait_for(pool, out_ready, i - 1)
                rstd_of(i % 2, 3)

        @block.scalar
        def _(act):
            n, r, g, p = Count(), Count(), Count(), Count()
            tr = [Count(), Count()]
            junk = ps[:, 6:8, :].rearrange("p a b -> p (a b)")

            def copy(dst, src, **kw):
                return act.activation(dst, src, ACT.Copy, **kw)

            def split(dst, elems=1024, cols=0, free=None):
                slot = n.slot(2)
                act.wait_ge(raw_landed[slot], n.rounds(2, 2 - KT // 2) * 16)
                if free:
                    wait_for(act, *free)
                src = raw[:, slot, 0:elems]
                copy(dst, src.rearrange("p (k c) -> p k c", c=cols) if cols else src).then_inc(w_hi, 1)
                n.next()

            def split_ring(free):
                split(ring[:, r.slot(2), HH, :], free=free)
                r.next()

            def split_next():
                split_ring((groups_done, g.at()))

            def transposed_hi(b, dst, blocks=4):
                wait_apart(act, act_passed, tr_done[b], tr[b].at(1))
                copy(dst, ps[:, TB[b], 0:P * blocks].rearrange("p (k t) -> p k t", t=P)).then_inc(tr_hi, 1)
                tr[b].next()

            def square_x(i):
                if i < 2:
                    act.wait_ge(x_first[i], 16)
                else:
                    act.wait_ge(x_landed[i % 2], 16 * (i // 2))
                wait_for(act, rstd_ready, i - 1)
                wait_for(act, squared, i)
                act.activation(junk, x_tile[:, i % 2, :], ACT.Square, accum_out=ssq[:, i % 2, 0:1])\
                    .then_inc(squared, 1)

            def x_hi(i):
                for b in range(2):
                    transposed_hi(b, xn[:, HH, 4 * b:4 * b + 4, P * i:P * (i + 1)])

            for b in range(2):
                act.dma_start(x_tile[:, b, :], x[0, P * b:P * (b + 1), :]).then_inc(x_first[b], 16)
            act.dma_start(g_pre_mix_b[:, :], g_pre_mix[0, :].partition_broadcast(P)).then_inc(g1_landed, 16)
            square_x(0)
            for m in range(KT):
                if m < KT // 2:
                    act.wait_ge(first_landed[m], 16)
                    copy(w_v[:, HH, :, P * m:P * (m + 1)], raw_first[:, m, :].rearrange("p (k c) -> p k c", c=P))\
                        .then_inc(w_hi, 1)
                    n.next()
                else:
                    split(w_v[:, HH, :, P * m:P * (m + 1)], cols=P)
                if m == 1:
                    square_x(1)
                if m == 3:
                    x_hi(0)
            for i in range(TT):
                if i + 1 < TT:
                    x_hi(i + 1)
                if i + 2 < TT:
                    square_x(i + 2)
                if i == 3:
                    act.wait_ge(lam_dots, 2)
                    act.activation(lam_exp[:, :], lam_dot[:, :], ACT.Exp).then_inc(lam_exps, 1)
                for half in range(2):
                    act.wait_ge(groups_done, g.at(1))
                    wait_for(act, v_stored[2 * (i % 2) + half], 16 * (i // 2))
                    copy(v_out[:, i % 2, half, :], ps[:, g.slot(4), :]).then_inc(evacuated[g.slot(4)], 1)
                    g.next()

            t, heads_in, heads_out = Count(), Count(), Count()

            def proj_hi_of(par, which, half):
                act.wait_ge(proj_done, p.at(1))
                copy((kt, qt)[which][:, par, HH, HALF * half:HALF * (half + 1)], ps[:, PROJ_BANK, :],
                     scale=(1.0, HD ** -0.5)[which]).then_inc(proj_hi, 1)
                p.next()

            def exps(i, c):
                w = P * (i + 1)
                act.wait_ge(max_ready, t.at() * 2 + (c + 1))
                wait_for(act, diff_ready, t.at(-1))
                act.activation(e_t[:, i % 2, c, 0:w],
                               ps[:, 2 * c:2 * c + 2, :].rearrange("p a b -> p (a b)")[:, 0:w], ACT.Exp,
                               bias=neg_max[:, i % 2, c:c + 1], accum_out=sums[:, i % 4, c:c + 1])\
                    .then_inc(exp_done, 1)

            def take_u_lo(i):
                act.wait_ge(pv_done, t.at(-1))
                wait_for(act, u_ready, t.at(-2))
                copy(u_lo[:, :], ps[:, U_BANK, HV:2 * HV]).then_inc(u_lo_ready, 1)

            def square_o(i):
                act.wait_ge(u_ready, t.at(-1))
                wait_for(act, o_scaled, t.at(-3))
                wait_for(act, o_squared, t.at(-2))
                act.activation(junk_o[:, :], u_row[:, i % 2, :], ACT.Square,
                               scale=rsums[:, i % 4, 0:1], accum_out=o_ssq[:, i % 2:i % 2 + 1])\
                    .then_inc(o_squared, 1)

            def y_hi(par, i):
                if i == 0:
                    heads_out.next()
                    act.wait_ge(y_free, heads_out.at())
                transposed_hi(1, y_out[:, par, HH, P * i:P * (i + 1)].rearrange("p (k t) -> p k t", t=P), 1)

            def split_v(par):
                act.wait_ge(v_landed, heads_in.at(1) * 16)
                wait_for(act, pv_done, heads_in.at(-1) * TT)
                copy(vh[:, par, HH], v_raw[:, :, :]).then_inc(v_hi, 1)
                heads_in.next()

            def step_of(par, i, lag=0, first=False, last=False):
                if not lag:
                    exps(i, 0)
                    exps(i, 1)
                if lag < 2 and not (first and i < 1):
                    wait_for(act, pv_done, t.at(-2))
                    before = (i - 1) % TT
                    for b in range(before // 4 + 1):
                        blocks = min(4, before + 1 - 4 * b)
                        transposed_hi(b, pt[:, before % 2, HH, 4 * b:4 * b + blocks, :], blocks)
                if not lag and not last:
                    if i in (2, 6):
                        split_ring((proj_done, p.at()))
                    if i == 4:
                        split_v(1 - par)
                    if i % 2 == 1:
                        proj_hi_of(1 - par, i // 4, i // 2 % 2)
                if lag < 3 and not (first and i < 2):
                    take_u_lo((i - 2) % TT)
                if not (first and i < 4):
                    y_hi(par if i >= 4 else 1 - par, (i - 4) % TT)
                if lag < 3 and not (first and i < 2):
                    square_o((i - 2) % TT)
                t.next()

            split_ring(None)
            split_ring(None)
            for half in range(2):
                proj_hi_of(0, 0, half)
            split_v(0)
            split_ring((proj_done, p.at()))
            for half in range(2):
                proj_hi_of(0, 1, half)
            for i in range(TT):
                step_of(0, i, first=True)
            with turns(act, (HEADS - 2) // 2, {n: 4, r: 4, p: 8, t: 16, tr[0]: 16, tr[1]: 24, heads_in: 2, heads_out: 2}):
                for par in (1, 0):
                    for i in range(TT):
                        step_of(par, i)
            for i in range(TT):
                step_of(1, i, last=True)
            for i in range(4):
                step_of(0, i, lag=i + 1)

            def sigmoid(dst, bias_col):
                for half in range(2):
                    wait_apart(act, act_passed, groups_done, g.at(1))
                    act.activation(dst(half), ps[:, g.slot(4), :], ACT.Sigmoid, bias=bias_col)\
                        .then_inc(evacuated[g.slot(4)], 1)
                    g.next()

            def tokens(buf, m):
                return lambda half: buf[:, bass.ds(m, 1), HALF * half:HALF * (half + 1)]\
                    .rearrange("p a t -> p (a t)")

            act.wait_ge(tr_free[1], TT + HEADS * (TT + TT // 2))
            act.wait_ge(small_landed, 16 * 5)
            with turns(act, KT // 2, {n: 2, r: 2, g: 4}) as it:
                for j in range(2):
                    split_next()
                    sigmoid(tokens(merged, it * 2 + j), bias_g[:, bass.ds(it * 2 + j, 1)])
            with turns(act, KT // 2, {n: 2, r: 2, g: 4}):
                for j in range(2):
                    split_next()
                    g.next(2)

            def take(dst):
                act.wait_ge(groups_done, g.at(1))
                copy(dst, ps[:, g.slot(4), :]).then_inc(evacuated[g.slot(4)], 1)
                g.next()

            def pool_out(c):
                for half in range(2):
                    act.wait_ge(groups_done, g.at(1))
                    copy(yp[:, HH, c, HALF * half:HALF * (half + 1)], ps[:, g.slot(4), :],
                         scale=scale_p[:, c:c + 1]).then_inc(yp_hi, 1)
                    g.next()

            for c in range(4):
                if c == 0:
                    split(w_pool[:, HH].rearrange("p g c -> p (g c)"), elems=512, free=(groups_done, g.at()))
                split_next()
                wait_for(act, d_ready, 2 * c)
                for half in range(2):
                    take(u_pad[:, 16 + HALF * half:16 + HALF * (half + 1)])
                if c >= 1:
                    pool_out(c - 1)
                act.wait_ge(d_ready, 2 * c + 2)
                copy(dh[:, HH, :], d_raw[:, :]).then_inc(d_hi, 1)

            for c in range(CT):
                split_next()
                if c > 0:
                    wait_evacuated(act, g, -3)
                for half in range(2):
                    take(conv_c[:, HALF * half:HALF * (half + 1)])
                split_next()
                g.next(2)
                if c == 0:
                    pool_out(3)
                split_next()
                for half in range(2):
                    wait_evacuated(act, g)
                    s = slice(HALF * half, HALF * (half + 1))
                    copy(yc[:, HH, c, s], y_raw[:, s]).then_inc(yc_hi, 1)
                    g.next()

            act.wait_ge(yc_lo, 2 * CT)
            with turns(act, KT // 4, {n: 6, r: 6, g: 16}) as it:
                for j in range(2):
                    for i in range(2):
                        split_next()
                        sigmoid(lambda half: gate[:, i, HALF * half:HALF * (half + 1)],
                                bias_g[:, bass.ds(it * 4 + (KT + 2 * j + i), 1)])
                    split_next()
                    g.next(4)

            with turns(act, KT // 2, {n: 2, r: 2, g: 4}) as it:
                for j in range(2):
                    split_next()
                    sigmoid(tokens(gate_c, it * 2 + j), bias_g[:, bass.ds(it * 2 + (2 * KT + j), 1)])
            for m2 in range(KT // 2):
                for m in (2 * m2, 2 * m2 + 1):
                    split(w_o[:, HH, :, P * m:P * (m + 1)], cols=P, free=(groups_done, g.at()))
                if m2 < KT // 2 - 1:
                    split_next()
                g.next(4)

            tile = Count()

            def merged_hi(i):
                wait_apart(act, act_passed, groups_done, g.at())
                copy(ring[:, r.slot(2), HH, :].rearrange("p (k t) -> p k t", t=P),
                     merged[:, :, bass.ds(i * P, P)]).then_inc(m_hi, 1)
                r.next()

            def hn_hi(i):
                for b in range(2):
                    transposed_hi(b, hn[:, HH, 4 * b:4 * b + 4, bass.ds(i * P, P)])

            def residual(b, i, first=False, last=False):
                if not last:
                    merged_hi(i + 1)
                act.wait_ge(groups_done, g.at(2))
                bank = g.slot(4)
                wait_for(act, x1_squared, tile.at())
                act.activation(junk, ps[:, bank:bank + 2, :].rearrange("p a b -> p (a b)"), ACT.Square,
                               accum_out=ssq[:, b, 1:2]).then_inc(squared, 1)
                g.next(2)
                if not first:
                    hn_hi(i - 1)
                act.wait_ge(x1_ready, tile.at(1))
                act.wait_ge(squared, tile.at(TT + 1))
                act.activation(junk, x1[:, b, :], ACT.Square, accum_out=ssq[:, b, 2:3]).then_inc(x1_squared, 1)
                tile.next()

            act.wait_ge(merged_ready, 2 * KT)
            merged_hi(0)
            residual(0, 0, first=True)
            with turns(act, (TT - 2) // 2, {r: 2, g: 4, tile: 2, tr[0]: 2, tr[1]: 2}) as it:
                residual(1, it * 2 + 1)
                residual(0, it * 2 + 2)
            split_next()
            residual(1, TT - 1, last=True)
            hn_hi(TT - 1)

            def ffn_chunk(par, last=False):
                for f in range(2):
                    split_next()
                    for half in range(2):
                        wait_evacuated(act, g, half - 2)
                    for half in range(2):
                        act.wait_ge(groups_done, g.at(1))
                        act.activation(silu[:, HALF * half:HALF * (half + 1)], ps[:, g.slot(4), :], ACT.Silu)\
                            .then_inc(evacuated[g.slot(4)], 1)
                        g.next()
                    if f == 0:
                        split_next()
                    else:
                        split(w_d[:, par, HH, 0, :], free=(groups_done, g.at()))
                    for half in range(2):
                        wait_evacuated(act, g)
                        s = slice(HALF * half, HALF * (half + 1))
                        copy(hf[:, par, HH, f, s], hf_raw[:, s]).then_inc(hf_hi, 1)
                        g.next()
                split(w_d[:, par, HH, 1, :], free=(groups_done, g.at()))
                if not last:
                    split_next()

            ffn_chunk(0)
            with turns(act, (FC - 3) // 2, {n: 12, r: 8, g: 48}):
                for par in (1, 0):
                    ffn_chunk(par)
                    g.next(16)
            ffn_chunk(1)
            g.next(16)
            ffn_chunk(0, last=True)
            for i in range(TT):
                for half in range(2):
                    wait_evacuated(act, g)
                    g.next()
                wait_for(act, rstd_ready, 3 * TT + i - 1)
                act.wait_ge(squared, 2 * TT + i)
                act.activation(junk, ff_sum[:, i, :], ACT.Square, accum_out=ssq[:, i % 2, 3:4])\
                    .then_inc(squared, 1)

        @block.vector
        def _(dve):
            n, r, g, p = Count(), Count(), Count(), Count()
            tr = [Count(), Count()]
            trs, step = Count(), Count()

            def did(ins):
                ins.then_inc(dve_step, 1)
                step.next()
                dve.wait_ge(dve_step, step.at())

            def lo(dst, src, hi):
                return dve.tensor_tensor(dst, src, hi.bitcast(F32), ALU.subtract)

            def split(buf, elems=1024, cols=0):
                slot = n.slot(2)
                dve.wait_ge(w_hi, n.at(1))
                src = raw[:, slot, 0:elems]
                lo(buf(LL), src.rearrange("p (k c) -> p k c", c=cols) if cols else src, buf(HH)).then_inc(w_lo, 1)
                n.next()

            def split_next():
                slot = r.slot(2)
                split(lambda s: ring[:, slot, s, :])
                r.next()

            def transposed_lo(b, buf, blocks=4):
                dve.wait_ge(tr_hi, trs.at(1))
                lo(buf(LL), ps[:, TB[b], 0:P * blocks].rearrange("p (k t) -> p k t", t=P), buf(HH))\
                    .then_inc(tr_free[b], 1)
                trs.next()

            def x_rows(i):
                dve.wait_ge(rstd_ready, i + 1)
                wait_for(dve, tr_done[1], i - 1)
                dve.scalar_tensor_tensor(xs_tile[:, i % 2, :], x_tile[:, i % 2, :], rstd[:, i % 2, 0:1],
                                         g_pre_mix_b[:, :], ALU.mult, ALU.mult).then_inc(rows_ready, 1)

            def x_lo(i):
                for b in range(2):
                    transposed_lo(b, lambda s: xn[:, s, 4 * b:4 * b + 4, P * i:P * (i + 1)])

            for m in range(KT):
                if m < KT // 2:
                    dve.wait_ge(w_hi, n.at(1))
                    s = slice(P * m, P * (m + 1))
                    lo(w_v[:, LL, :, s], raw_first[:, m, :].rearrange("p (k c) -> p k c", c=P), w_v[:, HH, :, s])\
                        .then_inc(w_lo, 1)
                    n.next()
                else:
                    split(lambda s: w_v[:, s, :, P * m:P * (m + 1)], cols=P)
                if m == 0:
                    dve.wait_ge(g1_landed, 16)
                    x_rows(0)
                if m == 2:
                    x_rows(1)
                if m == 3:
                    x_lo(0)
            for i in range(TT):
                if i + 1 < TT:
                    x_lo(i + 1)
                if i + 2 < TT:
                    x_rows(i + 2)
                if i == 2:
                    dve.wait_ge(lam_landed, 16 * 5)
                    for j in range(2):
                        did(dve.tensor_tensor(lam_in[:, 2 * j, :], lam_in[:, 2 * j, :], lam_in[:, 2 * j + 1, :],
                                              ALU.mult))
                        dve.tensor_reduce(lam_dot[:, j:j + 1], lam_in[:, 2 * j, :], AX_X, ALU.add)\
                            .then_inc(lam_dots, 1)
                if i == 4:
                    dve.wait_ge(lam_exps, 1)
                    did(dve.tensor_tensor(neg_lam[:, :], lam_exp[:, 1:2], lam_exp[:, 0:1], ALU.subtract))
                    did(dve.tensor_scalar(neg_lam[:, :], neg_lam[:, :], -LAMBDA_INIT, None, ALU.add))
                    did(dve.tensor_scalar(g_sub[:, :], g_sub[:, :], 1.0 - LAMBDA_INIT, None, ALU.mult))
                g.next(2)

            t = Count()

            def proj_lo_of(par, which, half):
                dve.wait_ge(proj_hi, p.at(1))
                buf, s = (kt, qt)[which], slice(HALF * half, HALF * (half + 1))
                dve.scalar_tensor_tensor(buf[:, par, LL, s], ps[:, PROJ_BANK, :], (1.0, HD ** -0.5)[which],
                                         buf[:, par, HH, s].bitcast(F32), ALU.mult, ALU.subtract)\
                    .then_inc(proj_lo, 1)
                p.next()

            heads_in = Count()

            def split_v(par):
                dve.wait_ge(v_hi, heads_in.at(1))
                lo(vh[:, par, LL], v_raw[:, :, :], vh[:, par, HH]).then_inc(v_lo, 1)
                heads_in.next()

            def difference(i):
                w, s, b = P * (i + 1), i % 4, i % 2
                dve.wait_ge(exp_done, t.at(1) * 2)
                did(dve.reciprocal(rsums[:, s, :], sums[:, s, :]))
                did(dve.tensor_scalar(d_scale[:, b:b + 1], sums[:, s, 0:1], rsums[:, s, 1:2], neg_lam[:, :],
                                      ALU.mult, ALU.mult))
                dve.scalar_tensor_tensor(diff[:, b, 0:w], e_t[:, b, 1, 0:w], d_scale[:, b:b + 1],
                                         e_t[:, b, 0, 0:w], ALU.mult, ALU.add).then_inc(diff_ready, 1)

            def maximum(i, c):
                dve.wait_ge(scores_done, t.at(1))
                dve.tensor_reduce(neg_max[:, i % 2, c:c + 1],
                                  ps[:, 2 * c:2 * c + 2, :].rearrange("p a b -> p (a b)")[:, 0:P * (i + 1)],
                                  AX_X, ALU.max, negate=True).then_inc(max_ready, 1)

            def y_of(i):
                dve.wait_ge(o_scaled, t.at(-2))
                dve.scalar_tensor_tensor(y_row[:, i % 2, :], u_row[:, i % 2, :],
                                         o_scale[:, i % 2:i % 2 + 1], g_sub[:, :], ALU.mult, ALU.mult)\
                    .then_inc(y_ready, 1)

            def sum_u(i):
                dve.wait_ge(u_lo_ready, t.at(-1))
                dve.tensor_tensor(u_row[:, i % 2, :], ps[:, U_BANK, 0:HV], u_lo[:, :], ALU.add).then_inc(u_ready, 1)

            def y_lo(par, i):
                transposed_lo(1, lambda s: y_out[:, par, s, P * i:P * (i + 1)].rearrange("p (k t) -> p k t", t=P), 1)

            def step_of(par, i, lag=0, first=False, last=False):
                if not lag:
                    maximum(i, 0)
                    maximum(i, 1)
                if lag < 4 and not (first and i < 3):
                    y_of((i - 3) % TT)
                if lag < 2 and not (first and i < 1):
                    before = (i - 1) % TT
                    for b in range(before // 4 + 1):
                        blocks = min(4, before + 1 - 4 * b)
                        transposed_lo(b, lambda s: pt[:, before % 2, s, 4 * b:4 * b + blocks, :], blocks)
                if not lag:
                    difference(i)
                if not lag and not last:
                    if i in (2, 6):
                        split_next()
                    if i == 4:
                        split_v(1 - par)
                    if i % 2 == 1:
                        proj_lo_of(1 - par, i // 4, i // 2 % 2)
                if lag < 3 and not (first and i < 2):
                    sum_u((i - 2) % TT)
                if not (first and i < 4):
                    y_lo(par if i >= 4 else 1 - par, (i - 4) % TT)
                t.next()

            split_next()
            split_next()
            for half in range(2):
                proj_lo_of(0, 0, half)
            split_v(0)
            split_next()
            for half in range(2):
                proj_lo_of(0, 1, half)
            for i in range(TT):
                step_of(0, i, first=True)
            with turns(dve, (HEADS - 2) // 2, {n: 4, r: 4, p: 8, t: 16, trs: 40, step: 32, heads_in: 2}):
                for par in (1, 0):
                    for i in range(TT):
                        step_of(par, i)
            for i in range(TT):
                step_of(1, i, last=True)
            for i in range(4):
                step_of(0, i, lag=i + 1)

            with turns(dve, KT // 2, {n: 2, r: 2, g: 4}):
                for j in range(2):
                    split_next()
                    g.next(2)
            with turns(dve, KT // 2, {n: 2, r: 2, g: 4}) as it:
                for j in range(2):
                    split_next()
                    for half in range(2):
                        dve.wait_ge(groups_done, g.at(1))
                        m = merged[:, bass.ds(it * 2 + j, 1), HALF * half:HALF * (half + 1)]\
                            .rearrange("p a t -> p (a t)")
                        dve.tensor_tensor(m, m, ps[:, g.slot(4), :], ALU.mult).then_inc(evacuated[g.slot(4)], 1)
                        g.next()

            def pool_d(c):
                w = WINDOWS[c]
                src, k = u_pad, 1
                for half in range(2):
                    wait_evacuated(dve, g, half)
                dve.wait_ge(pads_ready, 4)
                for dst in (sum_a, sum_b, sum_a, sum_b)[:c + 1]:
                    did(dve.tensor_tensor(dst[:, 16:16 + S], src[:, 16:16 + S], src[:, 16 - k:16 + S - k], ALU.add))
                    src, k = dst, 2 * k
                assert k == w
                wait_for(dve, d_hi, c)
                did(dve.tensor_tensor(first_w[:, 0:w], src[:, 16:16 + w], over_t[:, 0:w], ALU.mult))
                dve.scalar_tensor_tensor(d_raw[:, w:S], src[:, 16 + w:16 + S], 1.0 / w, u_pad[:, 16 + w:16 + S],
                                         ALU.mult, ALU.subtract).then_inc(d_ready, 1)
                dve.tensor_tensor(d_raw[:, 0:w], first_w[:, 0:w], u_pad[:, 16:16 + w], ALU.subtract)\
                    .then_inc(d_ready, 1)

            def pool_out(c):
                for half in range(2):
                    dve.wait_ge(yp_hi, 2 * c + half + 1)
                    s = slice(HALF * half, HALF * (half + 1))
                    dve.scalar_tensor_tensor(yp[:, LL, c, s], ps[:, g.slot(4), :], scale_p[:, c:c + 1],
                                             yp[:, HH, c, s].bitcast(F32), ALU.mult, ALU.subtract)\
                        .then_inc(evacuated[g.slot(4)], 1)
                    g.next()

            dve.wait_ge(small_landed, 16 * 5)
            dve.wait_ge(over_ready, 16)
            for c in range(4):
                if c == 0:
                    split(lambda s: w_pool[:, s].rearrange("p g c -> p (g c)"), elems=512)
                split_next()
                pool_d(c)
                g.next(2)
                if c >= 1:
                    pool_out(c - 1)
                dve.wait_ge(d_hi, c + 1)
                lo(dh[:, LL, :], d_raw[:, :], dh[:, HH, :]).then_inc(d_lo, 1)

            for c in range(CT):
                split_next()
                g.next(2)
                split_next()
                for half in range(2):
                    wait_evacuated(dve, g, -2)
                    dve.wait_ge(groups_done, g.at(1))
                    dve.tensor_tensor(conv_in[:, 2 + HALF * half:2 + HALF * (half + 1)], ps[:, g.slot(4), :],
                                      conv_c[:, HALF * half:HALF * (half + 1)], ALU.mult)\
                        .then_inc(evacuated[g.slot(4)], 1)
                    g.next()
                for half in range(2):
                    wait_evacuated(dve, g, half - 2)
                if c == 0:
                    pool_out(3)
                did(dve.tensor_scalar(conv_sum[:, :], conv_in[:, 0:S], conv_k[:, 0, c:c + 1], None, ALU.mult))
                for k in (1, 2):
                    did(dve.scalar_tensor_tensor(conv_sum[:, :], conv_in[:, k:k + S], conv_k[:, k, c:c + 1],
                                                 conv_sum[:, :], ALU.mult, ALU.add))
                split_next()
                for half in range(2):
                    dve.wait_ge(groups_done, g.at(1))
                    wait_for(dve, yc_hi, 2 * c)
                    s = slice(HALF * half, HALF * (half + 1))
                    dve.tensor_tensor(y_raw[:, s], ps[:, g.slot(4), :], conv_sum[:, s], ALU.mult)\
                        .then_inc(evacuated[g.slot(4)], 1)
                    g.next()
                for half in range(2):
                    dve.wait_ge(yc_hi, 2 * c + half + 1)
                    s = slice(HALF * half, HALF * (half + 1))
                    lo(yc[:, LL, c, s], y_raw[:, s], yc[:, HH, c, s]).then_inc(yc_lo, 1)

            with turns(dve, KT // 4, {n: 6, r: 6, g: 16}) as it:
                for j in range(2):
                    for i in range(2):
                        split_next()
                        g.next(2)
                    split_next()
                    for i in range(2):
                        for half in range(2):
                            dve.wait_ge(groups_done, g.at(1))
                            bank = g.slot(4)
                            s = slice(HALF * half, HALF * (half + 1))
                            dve.tensor_tensor(gated[:, half, :], gate[:, i, s], ps[:, bank, :], ALU.mult)\
                                .then_inc(evacuated[bank], 1)
                            wait_evacuated(dve, g)
                            m = merged[:, bass.ds(it * 4 + (2 * j + i), 1), s].rearrange("p a t -> p (a t)")
                            dve.tensor_tensor(m, m, gated[:, half, :], ALU.add)
                            g.next()

            with turns(dve, KT // 2, {n: 2, r: 2, g: 4}):
                for j in range(2):
                    split_next()
                    g.next(2)
            for m2 in range(KT // 2):
                for m in (2 * m2, 2 * m2 + 1):
                    split(lambda s: w_o[:, s, :, P * m:P * (m + 1)], cols=P)
                if m2 < KT // 2 - 1:
                    split_next()
                for m in (2 * m2, 2 * m2 + 1):
                    for half in range(2):
                        dve.wait_ge(groups_done, g.at(1))
                        s = slice(HALF * half, HALF * (half + 1))
                        dve.tensor_tensor(gate_c[:, m, s], gate_c[:, m, s], ps[:, g.slot(4), :], ALU.mult)\
                            .then_inc(evacuated[g.slot(4)], 1)
                        wait_evacuated(dve, g)
                        dve.tensor_tensor(merged[:, m, s], merged[:, m, s], gate_c[:, m, s], ALU.add)\
                            .then_inc(merged_ready, 1)
                        g.next()

            tile = Count()

            def merged_lo(i):
                slot = r.slot(2)
                dve.wait_ge(m_hi, r.at(1 - m_first))
                lo(ring[:, slot, LL, :].rearrange("p (k t) -> p k t", t=P), merged[:, :, bass.ds(i * P, P)],
                   ring[:, slot, HH, :].rearrange("p (k t) -> p k t", t=P)).then_inc(m_lo, 1)
                r.next()

            def hn_lo(i):
                for b in range(2):
                    transposed_lo(b, lambda s: hn[:, s, 4 * b:4 * b + 4, bass.ds(i * P, P)])

            def residual(b, i, first=False, last=False):
                if not last:
                    merged_lo(i + 1)
                if not first:
                    dve.wait_ge(tr_done[1], tile.at(tr_first))
                dve.wait_ge(rstd_ready, tile.at() * 2 + (TT + 1))
                for half in range(2):
                    s = slice(HALF * half, HALF * (half + 1))
                    dve.scalar_tensor_tensor(row[:, s], ps[:, g.slot(4), :], rstd[:, b, 1:2], g_post_mix_b[:, s],
                                             ALU.mult, ALU.mult).then_inc(evacuated[g.slot(4)], 1)
                    g.next()
                for half in range(2):
                    wait_evacuated(dve, g, half - 2)
                dve.wait_ge(x_landed[b], tile.rounds(2, TT) * 16)
                dve.tensor_tensor(x1[:, b, :], x1[:, b, :], row[:, :], ALU.add).then_inc(x1_ready, 1)
                if not first:
                    hn_lo(i - 1)
                dve.wait_ge(rstd_ready, tile.at() * 2 + (TT + 2))
                dve.wait_ge(x1_ready, tile.at(1))
                dve.scalar_tensor_tensor(row[:, :], x1[:, b, :], rstd[:, b, 2:3], g_pre_ffn_b[:, :],
                                         ALU.mult, ALU.mult).then_inc(hn_rows, 1)
                tile.next()

            m_first = r.first
            tr_first = TT + HEADS * (TT + TT // 2)
            dve.wait_ge(g2_landed, 32)
            merged_lo(0)
            residual(0, 0, first=True)
            with turns(dve, (TT - 2) // 2, {r: 2, g: 4, tile: 2, trs: 4}) as it:
                residual(1, it * 2 + 1)
                residual(0, it * 2 + 2)
            split_next()
            residual(1, TT - 1, last=True)
            hn_lo(TT - 1)

            u = Count()

            def ffn_chunk(par, last=False):
                for f in range(2):
                    split_next()
                    g.next(2)
                    if f == 0:
                        split_next()
                    else:
                        split(lambda s: w_d[:, par, s, 0, :])
                    for half in range(2):
                        wait_evacuated(dve, g, -2)
                        dve.wait_ge(groups_done, g.at(1))
                        wait_for(dve, hf_hi, u.at(half - 1))
                        s = slice(HALF * half, HALF * (half + 1))
                        dve.tensor_tensor(hf_raw[:, s], silu[:, s], ps[:, g.slot(4), :], ALU.mult)\
                            .then_inc(evacuated[g.slot(4)], 1)
                        g.next()
                    for half in range(2):
                        dve.wait_ge(hf_hi, u.at(half + 1))
                        s = slice(HALF * half, HALF * (half + 1))
                        lo(hf[:, par, LL, f, s], hf_raw[:, s], hf[:, par, HH, f, s]).then_inc(hf_lo, 1)
                    u.next(2)
                split(lambda s: w_d[:, par, s, 1, :])
                if not last:
                    split_next()

            def add_down():
                for i in range(TT):
                    for half in range(2):
                        dve.wait_ge(groups_done, g.at(1))
                        f = ff_sum[:, i, HALF * half:HALF * (half + 1)]
                        dve.tensor_tensor(f, f, ps[:, g.slot(4), :], ALU.add).then_inc(evacuated[g.slot(4)], 1)
                        g.next()

            ffn_chunk(0)
            dve.wait_ge(sum_zero, TT)
            with turns(dve, (FC - 3) // 2, {n: 12, r: 8, g: 48, u: 8}):
                for par in (1, 0):
                    ffn_chunk(par)
                    add_down()
            ffn_chunk(1)
            add_down()
            ffn_chunk(0, last=True)

            def finish(i):
                b = i % 2
                dve.wait_ge(rstd_ready, 3 * TT + i + 1)
                did(dve.scalar_tensor_tensor(ff_sum[:, i, :], ff_sum[:, i, :], rstd[:, b, 3:4], g_post_ffn_b[:, :],
                                             ALU.mult, ALU.mult))
                dve.tensor_tensor(out_t[:, i, :], x1_again[:, i, :], ff_sum[:, i, :], ALU.add)\
                    .then_inc(out_ready, 1)

            for i in range(TT):
                for half in range(2):
                    dve.wait_ge(groups_done, g.at(1))
                    f = ff_sum[:, i, HALF * half:HALF * (half + 1)]
                    dve.tensor_tensor(f, f, ps[:, g.slot(4), :], ALU.add).then_inc(evacuated[g.slot(4)], 1)
                    g.next()
                if i == 0:
                    dve.wait_ge(g3_landed, 16)
                    dve.wait_ge(x1_landed, 16 * TT)
                else:
                    finish(i - 1)
            finish(TT - 1)

        @block.tensor
        def _(pe):
            n, r, g, p = Count(), Count(), Count(), Count()
            tr = [Count(), Count()]

            def job_weights():
                pe.wait_ge(w_lo, n.at(1))
                n.next()

            def group(operands, out_w=HALF):
                bank = g.slot(4)
                if g.first >= 4:
                    wait_evacuated(pe, g, -4)
                pairs = list(operands)
                for i, (lhs, rhs) in enumerate(pairs):
                    last = pe.matmul(ps[:, bank, :], lhs, rhs, start=i == 0, stop=i == len(pairs) - 1)
                last.then_inc(groups_done, 1)
                g.next()

            def transpose_rows(b, src, blocks=4):
                wait_for(pe, tr_free[b], tr[b].at())
                for k in range(blocks):
                    last = pe.transpose(ps[:, TB[b], P * k:P * (k + 1)], src[:, P * k:P * (k + 1)], ident[:, :])
                last.then_inc(tr_done[b], 1)
                tr[b].next()

            def job(moving, cols=P, blocks=KT):
                job_weights()
                slot = r.slot(2)
                w = ring[:, slot].rearrange("p s (k c) -> p s k c", c=cols)
                for m in range(cols // P):
                    for half in range(2):
                        group((w[:, a, k, P * m:P * (m + 1)], moving[:, b, k, HALF * half:HALF * (half + 1)])
                              for k in range(blocks) for a, b in PASSES)
                r.next()

            def x_transposed(i):
                pe.wait_ge(rows_ready, i + 1)
                for b in range(2):
                    transpose_rows(b, xs_tile[:, i % 2, HALF * b:HALF * (b + 1)])

            pe.wait_ge(ident_ready, 1)
            x_transposed(0)
            for i in range(TT):
                if i + 1 < TT:
                    x_transposed(i + 1)
                for b in range(2):
                    pe.wait_ge(tr_free[b], i + 1)
                for half in range(2):
                    if i == 0:
                        pe.wait_ge(w_lo, 4 * (half + 1))
                    group((xn[:, a, k, P * i:P * (i + 1)], w_v[:, b, k, HALF * half:HALF * (half + 1)])
                          for k in range(KT) for a, b in PASSES)
            n.next(KT)

            t = Count()
            heads_v = Count()

            def proj_part(which, part):
                half, ks = part // 2, range(4 * (part % 2), 4 * (part % 2) + 4)
                if part == 0:
                    job_weights()
                if part % 2 == 0:
                    wait_for(pe, proj_lo, p.at())
                for k in ks:
                    for a, b in PASSES:
                        last = pe.matmul(ps[:, PROJ_BANK, :], ring[:, which, a, P * k:P * (k + 1)],
                                         xn[:, b, k, HALF * half:HALF * (half + 1)],
                                         start=(k == 0 and (a, b) == PASSES[0]),
                                         stop=(k == KT - 1 and (a, b) == PASSES[-1]))
                if part % 2 == 1:
                    last.then_inc(proj_done, 1)
                    p.next()

            def scores(par, i):
                wait_for(pe, exp_done, t.at() * 2)
                for chunk in range(i // 4 + 1):
                    w = min(HALF, P * (i + 1) - HALF * chunk)
                    for n_pass, (a, b) in enumerate(PASSES):
                        for c in range(2):
                            rows = slice(HD * c, HD * (c + 1))
                            if n_pass == 2 and chunk == i // 4:
                                for m in range(2):
                                    o = P * (i % 4) + 64 * m
                                    pe.matmul(ps[:, 2 * c + chunk, o:P * (i % 4 + 1)], select[rows, m, :],
                                              mask[rows, m, 64 * m:P], start=False, stop=False)
                            last = pe.matmul(ps[:, 2 * c + chunk, 0:w], qt[rows, par, a, P * i:P * (i + 1)],
                                             kt[rows, par, b, HALF * chunk:HALF * chunk + w],
                                             start=n_pass == 0, stop=n_pass == 2)
                last.then_inc(scores_done, 1)

            def diff_transposed(i):
                pe.wait_ge(diff_ready, t.at())
                for b in range(i // 4 + 1):
                    blocks = min(4, i + 1 - 4 * b)
                    transpose_rows(b, diff[:, i % 2, HALF * b:HALF * b + P * blocks], blocks)

            def weighted_values(par, i, newer):
                if i == 0:
                    pe.wait_ge(v_lo, heads_v.at(1))
                    heads_v.next()
                for b in range(i // 4 + 1):
                    pe.wait_ge(tr_free[b], tr[b].at(-newer[b]))
                wait_for(pe, u_ready, t.at(-2))
                for k in range(i + 1):
                    pe.matmul(ps[:, U_BANK, 0:2 * HV], pt[:, i % 2, HH, k, :], vh[:, par, :, k, :],
                              start=k == 0, stop=k == i, skip_group_check=True)
                    last = pe.matmul(ps[:, U_BANK, 0:HV], pt[:, i % 2, LL, k, :], vh[:, par, HH, k, :],
                                     start=False, stop=k == i, skip_group_check=True)
                last.then_inc(pv_done, 1)

            def y_transposed(i):
                pe.wait_ge(y_ready, t.at(-3))
                transpose_rows(1, y_row[:, i % 2, :], 1)

            def step_of(par, i, lag=0, first=False, last=False):
                if not lag:
                    if i == 0:
                        pe.wait_ge(proj_lo, p.at(-1))
                    if i == 4:
                        pe.wait_ge(proj_lo, p.at(-(2 if not last else 0)))
                    scores(par, i)
                newer = (0, 0)
                if lag < 2 and not (first and i < 1):
                    before = (i - 1) % TT
                    diff_transposed(before)
                    newer = (1, before // 4)
                if not lag and not last:
                    proj_part(i // 4, i % 4)
                if lag < 3 and not (first and i < 2):
                    weighted_values(par if i >= 2 else 1 - par, (i - 2) % TT, newer)
                if lag < 5 and not (first and i < 4):
                    y_transposed((i - 4) % TT)
                t.next()

            for which in range(2):
                for part in range(4):
                    proj_part(which, part)
            for b in range(4):
                wait_evacuated(pe, g, b - 4)
            pe.wait_ge(mask_ready, 4)
            for i in range(TT):
                step_of(0, i, first=True)
            with turns(pe, (HEADS - 2) // 2, {n: 4, p: 8, t: 16, tr[0]: 16, tr[1]: 24, heads_v: 2}):
                for par in (1, 0):
                    for i in range(TT):
                        step_of(par, i)
            for i in range(TT):
                step_of(1, i, last=True)
            for i in range(4):
                step_of(0, i, lag=i + 1)
            pe.wait_ge(exp_done, 2 * HEADS * TT)
            r.next(2 * HEADS)

            with turns(pe, KT // 2, {n: 2, r: 2, g: 4}):
                for j in range(2):
                    job(xn)
            pe.wait_ge(y_landed, 16 * HEADS)
            with turns(pe, KT // 2, {n: 2, r: 2, g: 4}):
                for j in range(2):
                    job(ya)

            def pool_group(c):
                pe.wait_ge(d_lo, c + 1)
                for half in range(2):
                    group((w_pool[:, a, c, :], dh[:, b, HALF * half:HALF * (half + 1)]) for a, b in PASSES)

            for c in range(4):
                job(xn)
                if c == 0:
                    n.next()
                else:
                    pool_group(c - 1)
            for c in range(CT):
                job(xn)
                job(xn)
                if c == 0:
                    pool_group(3)
                job(xn)
            pe.wait_ge(yc_lo, 2 * CT)
            with turns(pe, KT // 4, {n: 6, r: 6, g: 16}):
                for j in range(2):
                    job(xn)
                    job(xn)
                    job(yc, 2 * P, CT)
            with turns(pe, KT // 2, {n: 2, r: 2, g: 4}):
                for j in range(2):
                    job(xn)
            for m2 in range(KT // 2):
                job(yp, 2 * P, CT)
                n.next(2)

            tile = Count()

            def mix():
                pe.wait_ge(m_lo, tile.at(1))
                slot = r.slot(2)
                for half in range(2):
                    group((ring[:, slot, a, P * k:P * (k + 1)], w_o[:, b, k, HALF * half:HALF * (half + 1)])
                          for k in range(KT) for a, b in PASSES)
                r.next()
                tile.next()

            def hn_transposed():
                pe.wait_ge(hn_rows, tile.at(-1))
                for b in range(2):
                    transpose_rows(b, row[:, HALF * b:HALF * (b + 1)])

            pe.wait_ge(w_lo, n.at())
            mix()
            with turns(pe, (TT - 2) // 2, {r: 2, g: 4, tile: 2, tr[0]: 2, tr[1]: 2}):
                for j in range(2):
                    mix()
                    hn_transposed()
            mix()
            hn_transposed()
            tile.next()
            hn_transposed()
            for b in range(2):
                pe.wait_ge(tr_free[b], tr[b].at())

            u = Count()

            def ffn_chunk():
                for f in range(2):
                    job(hn)
                    job(hn)
                n.next(2)
                u.next(4)

            def down(pars, newer):
                pe.wait_ge(w_lo, n.at(-newer))
                pe.wait_ge(hf_lo, u.at(-4 if newer else 0))
                for i in range(TT):
                    for half in range(2):
                        group((hf[:, par, a, f, P * i:P * (i + 1)], w_d[:, par, b, f, HALF * half:HALF * (half + 1)])
                              for par in pars for f in range(2) for a, b in PASSES)

            ffn_chunk()
            with turns(pe, (FC - 3) // 2, {n: 12, r: 8, g: 48, u: 8}):
                for par in (1, 0):
                    ffn_chunk()
                    down((1 - par,), 6)
            ffn_chunk()
            down((0,), 6)
            ffn_chunk()
            down((1, 0), 0)
            assert g.first == GROUPS


_INS = ["x", "g_pre_mix", "w_in", "b_gate", "lambda_q1", "lambda_k1", "lambda_q2", "lambda_k2", "subln_g",
        "w_attn_proj", "conv_w", "w_conv_proj", "pool_w", "pool_scale", "w_pool_proj", "w_out", "g_post_mix",
        "g_pre_ffn", "w_gate_up", "w_down", "g_post_ffn"]


def kernel(**inputs):
    import numpy as _np
    import concourse.bacc as _bacc
    from concourse import mybir as _mybir
    from concourse.bass_utils import run_bass_kernel_spmd as _run

    nc = _bacc.Bacc("TRN2", target_bir_lowering=False, num_devices=1)
    arrays, args = {}, []
    for name in _INS:
        a = _np.ascontiguousarray(inputs[name])
        arrays[f"in_{name}_dram"] = a
        args.append(nc.dram_tensor(f"in_{name}_dram", a.shape, _mybir.dt.from_np(a.dtype), kind="ExternalInput").ap())
    shape = arrays["in_x_dram"].shape
    args.append(nc.dram_tensor("out_0_dram", shape, _mybir.dt.float32, kind="ExternalOutput").ap())
    build(nc, *args)
    r = _run(nc, [arrays], core_ids=[0])
    return r.results[0]["out_0_dram"]
```

```python
import math
from contextlib import ExitStack, contextmanager

import concourse.bass as bass
from concourse import mybir

F32 = mybir.dt.float32
F32R = mybir.dt.float32r
ALU = mybir.AluOpType
ACT = mybir.ActivationFunctionType
AX_X = mybir.AxisListType.X

P = 128
HALF = 512
EPS = 1e-6
MASKED = -1e30
WINDOWS = (2, 4, 8, 16)
HH, LL = 0, 1
PASSES = ((HH, HH), (HH, LL), (LL, HH))


class Count:

    def __init__(self):
        self.first, self.step, self.turn = 0, 0, 0

    def at(self, plus=0):
        v = self.first + plus
        return self.turn * self.step + v if self.step else v

    def slot(self, ring, plus=0):
        assert self.step % ring == 0
        return (self.first + plus) % ring

    def rounds(self, ring, plus=0):
        v = (self.first + plus) // ring
        return self.turn * (self.step // ring) + v if self.step else v

    def next(self, by=1):
        self.first += by


@contextmanager
def turns(eng, n, advance):
    before = {c: c.first for c in advance}
    with eng.Fori(0, n) as turn:
        for c, step in advance.items():
            c.step, c.turn = step, turn
        yield turn
        for c, step in advance.items():
            assert c.first - before[c] == step, (c.first - before[c], step)
            c.first, c.step, c.turn = before[c] + n * step, 0, 0


def wait_for(eng, sem, value):
    if not isinstance(value, int) or value > 0:
        eng.wait_ge(sem, value)


def wait_apart(eng, passed, sem, value):
    wait_for(eng, sem, value)
    if not isinstance(value, int):
        eng.sem_inc(passed, 1)


def build(nc, x, g_pre_mix, w_in, b_gate, lambda_q1, lambda_k1, lambda_q2, lambda_k2, subln_g,
          w_attn_proj, conv_w, w_conv_proj, pool_w, pool_scale, w_pool_proj, w_out, g_post_mix,
          g_pre_ffn, w_gate_up, w_down, g_post_ffn, out):
    _, S, D = x.shape
    HD = lambda_q1.shape[1]
    HV = 2 * HD
    HEADS = w_attn_proj.shape[1] // HV
    CW = conv_w.shape[2]
    CT = CW // P
    KT = D // P
    TT = S // P
    FF = w_down.shape[1]
    FT = FF // P
    FC = FT // 2
    LAMBDA_INIT = 0.8 - 0.6 * math.exp(-0.3 * 0)
    assert S == D == 2 * HALF and KT == TT == HEADS == 8 and HV == P and CT == len(WINDOWS) == 4 and FC == 11
    OFF_Q, OFF_K, OFF_V = 0, D, 2 * D
    OFF_CB = 3 * D
    OFF_CC, OFF_CH, OFF_POOL = OFF_CB + CW, OFF_CB + 2 * CW, OFF_CB + 3 * CW
    OFF_GATE = OFF_POOL + len(WINDOWS) * P
    GROUPS = 2 * TT + 4 * (KT - 1) + 4 * 4 + 6 * CT + 4 * KT + 4 * KT + 2 * TT + 8 * FC + 2 * TT * (FC - 1)

    ctx = ExitStack()
    with ctx:
        def sem(name):
            return ctx.enter_context(nc.semaphore(name))

        BASE = 16512
        R1 = BASE
        R2 = R1 + 65536
        R2B = R2 + 32768
        RF = R2 + 65536
        RRAW = RF + 32768
        RRING = RRAW + 8192
        RT = RRING + 16384
        RM = RT + 4096
        RC = RM + 4 * 4096 + 32
        consts_at = [RC]

        def at(name, shape, dt, offset):
            return nc.alloc_sbuf_tensor_at(name, shape, dt, offset=offset)

        def const(name, shape, dt=F32):
            size = math.prod(shape[1:]) * 4
            t = at(name, shape, dt, consts_at[0])
            consts_at[0] += (size + 31) // 32 * 32
            return t

        xn = at("xn", [P, 2, KT, S], F32R, R1)
        w_o = at("w_o", [P, 2, KT, D], F32R, R1)
        ff_sum = at("ff_sum", [P, TT, D], F32, R1)
        hf = at("hf", [P, 2, 2, 2, S], F32R, R1 + 32768)

        w_v = at("w_v", [P, 2, KT, D], F32R, R2)
        qt = at("qt", [P, 2, 2, S], F32R, R2)
        kt = at("kt", [P, 2, 2, S], F32R, R2 + 16384)
        vh = at("vh", [P, 2, 2, TT, HV], F32R, R2 + 32768)
        pt = at("pt", [P, 2, 2, TT, P], F32R, R2 + 49152)
        ya = at("ya", [P, 2, HEADS, S], F32R, R2)
        u_pad = at("u_pad", [P, 16 + S], F32, R2)
        sum_a = at("sum_a", [P, 16 + S], F32, R2 + 4160)
        sum_b = at("sum_b", [P, 16 + S], F32, R2 + 8320)
        d_raw = at("d_raw", [P, S], F32, R2 + 12480)
        dh = at("dh", [P, 2, S], F32R, R2 + 16576)
        w_pool = at("w_pool", [P, 2, 4, P], F32R, R2 + 24768)
        yc = at("yc", [P, 2, CT, S], F32R, R2)
        gate_c = at("gate_c", [P, KT, S], F32, R2)
        yp = at("yp", [P, 2, CT, S], F32R, R2B)
        hn = at("hn", [P, 2, KT, S], F32R, R2)

        x_tile = at("x_tile", [P, 2, D], F32, RF)
        xs_tile = at("xs_tile", [P, 2, D], F32, RF + 8192)
        g_pre_mix_b = at("g_pre_mix_b", [P, D], F32, RF + 16384)
        v_out = at("v_out", [P, 2, 2, HALF], F32, RF + 20480)
        e_t = at("e_t", [P, 2, 2, S], F32, RF)
        diff = at("diff", [P, 2, S], F32, RF + 16384)
        gates_raw = at("gates_raw", [P, 2, S], F32, R2 + 16384)
        v_raw = at("v_raw", [P, TT, HV], F32, RF + 24576)
        y_row = at("y_row", [P, 2, HV], F32, RF + 28672)
        junk_o = at("junk_o", [P, HV], F32, RF + 28672 + 1024)
        u_lo = at("u_lo", [P, HV], F32, RF + 28672 + 1536)
        u_row = at("u_row", [P, 2, HV], F32, RF + 28672 + 2048)
        merged = at("merged", [P, KT, S], F32, RF)
        w_d = at("w_d", [P, 2, 2, 2, D], F32R, RF)

        raw_first = at("raw_first", [P, KT // 2, 1024], F32, RM)
        raw_last = at("raw_last", [P, KT // 4, 1024], F32, RRING)
        raw = at("raw", [P, 2, 1024], F32, RRAW)
        ring = at("ring", [P, 2, 2, 1024], F32R, RRING)

        y_out = at("y_out", [P, 2, 2, S], F32R, RM)
        gate = at("gate", [P, 2, S], F32, RM)
        gated = at("gated", [P, 2, HALF], F32, RM + 8192)
        conv_c = at("conv_c", [P, S], F32, RM)
        conv_in = at("conv_in", [P, 2 + S], F32, RM + 4096)
        conv_sum = at("conv_sum", [P, S], F32, RM + 8224)
        y_raw = at("y_raw", [P, S], F32, RM + 12320)
        g_post_mix_b = at("g_post_mix_b", [P, D], F32, RM)
        g_pre_ffn_b = at("g_pre_ffn_b", [P, D], F32, RM + 4096)
        x1 = at("x1", [P, 2, D], F32, RM + 8192)
        row = at("row", [P, D], F32, RT)
        silu = at("silu", [P, S], F32, RM)
        hf_raw = at("hf_raw", [P, S], F32, RM + 4096)
        g_post_ffn_b = at("g_post_ffn_b", [P, D], F32, RM)
        x1_again = at("x1_again", [P, TT, D], F32, R2)
        out_t = at("out_t", [P, TT, D], F32, R2B)

        ident = const("ident", [P, P])
        mask = const("mask", [P, 2, P])
        bias_g = const("bias_g", [P, 3 * KT])
        conv_k = const("conv_k", [P, 3, CT])
        scale_p = const("scale_p", [P, CT])
        over_t = const("over_t", [P, 16])
        first_w = const("first_w", [P, 16])
        g_sub = const("g_sub", [P, HV])
        minus_half = const("minus_half", [P, 1])
        ssq = const("ssq", [P, 2, 4])
        rstd = const("rstd", [P, 2, 4])
        lam_in = const("lam_in", [P, 4, HD])
        lam_dot = const("lam_dot", [P, 2])
        lam_exp = const("lam_exp", [P, 2])
        neg_lam = const("neg_lam", [P, 1])
        neg_max = const("neg_max", [P, 2, 2])
        sums = const("sums", [P, 4, 2])
        rsums = const("rsums", [P, 4, 2])
        d_scale = const("d_scale", [P, 2])
        o_ssq = const("o_ssq", [P, 2])
        o_scale = const("o_scale", [P, 2])
        assert consts_at[0] <= 229344, consts_at[0]

        ps = ctx.enter_context(nc.psum_tensor("ps", [P, 8, 512], F32))
        TB = (4, 5)
        U_BANK, PROJ_BANK = 6, 7

        def proj_bank(first, part):
            return (U_BANK, PROJ_BANK)[part % 2] if first else PROJ_BANK

        v_dram = nc.dram_tensor("v_scratch", (S, D), F32).ap()
        y_dram = nc.dram_tensor("y_scratch", (HEADS, P, 2 * S), F32).ap()
        x1_dram = nc.dram_tensor("x1_scratch", (S, D), F32).ap()

        raw_landed = [sem(f"raw_landed{i}") for i in range(2)]
        first_landed = [sem(f"first_landed{i}") for i in range(KT)]
        w_hi, w_lo = sem("w_hi"), sem("w_lo")
        groups_done = sem("groups_done")
        evacuated = [sem(f"evacuated{i}") for i in range(4)]
        tr_done = [sem(f"tr_done{i}") for i in range(2)]
        tr_free = [sem(f"tr_free{i}") for i in range(2)]
        tr_hi = sem("tr_hi")
        ident_ready, half_ready, mask_ready = sem("ident_ready"), sem("half_ready"), sem("mask_ready")
        small_landed, lam_landed, over_ready = sem("small_landed"), sem("lam_landed"), sem("over_ready")
        g1_landed, g2_landed, g3_landed = sem("g1_landed"), sem("g2_landed"), sem("g3_landed")
        x_first = [sem(f"x_first{i}") for i in range(2)]
        gates_first = sem("gates_first")
        x_landed = [sem(f"x_landed{i}") for i in range(2)]
        squared, rstd_ready, rows_ready = sem("squared"), sem("rstd_ready"), sem("rows_ready")
        sp_passed, act_passed, pool_passed = sem("sp_passed"), sem("act_passed"), sem("pool_passed")
        pool_step, dve_step = sem("pool_step"), sem("dve_step")
        v_stored = [sem(f"v_stored{i}") for i in range(4)]
        lam_dots, lam_exps = sem("lam_dots"), sem("lam_exps")
        v_landed, v_hi, v_lo = sem("v_landed"), sem("v_hi"), sem("v_lo")
        proj_done, proj_hi, proj_lo = sem("proj_done"), sem("proj_hi"), sem("proj_lo")
        scores_done, max_ready, exp_done = sem("scores_done"), sem("max_ready"), sem("exp_done")
        diff_ready = sem("diff_ready")
        u_lo_ready, u_ready = sem("u_lo_ready"), sem("u_ready")
        pv_done, o_squared, o_scaled, y_ready = sem("pv_done"), sem("o_squared"), sem("o_scaled"), sem("y_ready")
        y_stored = [sem(f"y_stored{i}") for i in range(2)]
        y_free, y_landed = sem("y_free"), sem("y_landed")
        pads_ready = sem("pads_ready")
        d_ready, d_hi, d_lo = sem("d_ready"), sem("d_hi"), sem("d_lo")
        yp_hi, yc_hi, yc_lo = sem("yp_hi"), sem("yc_hi"), sem("yc_lo")
        merged_ready = sem("merged_ready")
        m_hi, m_lo = sem("m_hi"), sem("m_lo")
        x1_ready, x1_squared, hn_rows = sem("x1_ready"), sem("x1_squared"), sem("hn_rows")
        x1_stored = [sem(f"x1_stored{i}") for i in range(2)]
        hf_hi, hf_lo = sem("hf_hi"), sem("hf_lo")
        sum_zero = sem("sum_zero")
        out_ready = sem("out_ready")
        out_stored = sem("out_stored")
        x1_landed = sem("x1_landed")

        C_ORDER = [((0, 0), (0, 1), (1, 0), (1, 1))] * (KT // 2 - 1) + [((0, 0), (1, 0), (0, 1), (1, 1))]

        def v_part(m):
            return slice(2 * (m % 4), 2 * (m % 4) + 2), slice(HALF * (m // 4), HALF * (m // 4) + HALF)

        def first_tile(m):
            return raw_first[:, m, :] if m < 4 else raw[:, m - 4, :] if m < 6 else raw_last[:, m - 6, :]

        def wait_evacuated(eng, g, plus=0):
            eng.wait_ge(evacuated[g.slot(4, plus)], g.rounds(4, plus + 4))

        block = ctx.enter_context(nc.Block())

        @block.sync
        def _(sp):
            n = Count()

            def load(src, cols=P):
                slot = n.slot(2)
                wait_apart(sp, sp_passed, w_lo, n.at(-1))
                dst = raw[:, slot, :]
                if cols:
                    dst = dst.rearrange("p (k c) -> p k c", c=cols)[:, 0:src.shape[1], :]
                sp.dma_start(dst, src).then_inc(raw_landed[slot], 16)
                n.next()

            def tile_of(w, first, cols=P):
                return w[0].rearrange("(k p) c -> p k c", p=P)[:, :, bass.ds(first, cols)]

            def v_tile(m):
                k, c = v_part(m)
                return w_in[0, 0:D, OFF_V + c.start:OFF_V + c.stop].rearrange("(k p) c -> p k c", p=P)[:, k, :]

            for m in range(KT):
                sp.dma_start(first_tile(m).rearrange("p (k c) -> p k c", c=HALF), v_tile(m))\
                    .then_inc(first_landed[m], 16)
                if m == 3:
                    sp.dma_start(x_tile[:, 1, :], x[0, P:2 * P, :]).then_inc(x_first[1], 16)
            n.next(KT)
            for h in range(2):
                load(tile_of(w_in, OFF_K + P * h))
                load(tile_of(w_in, OFF_Q + P * h))
            with turns(sp, (HEADS - 2) // 2, {n: 4}) as it:
                for j in range(2):
                    load(tile_of(w_in, it * (2 * P) + (OFF_K + P * (2 + j))))
                    load(tile_of(w_in, it * (2 * P) + (OFF_Q + P * (2 + j))))
            with turns(sp, KT // 2, {n: 2}) as it:
                for j in range(2):
                    load(tile_of(w_in, it * (2 * P) + (OFF_GATE + P * j)))
            with turns(sp, KT // 2, {n: 2}) as it:
                for j in range(2):
                    load(tile_of(w_attn_proj, it * (2 * P) + P * j))
            for c in range(4):
                load(tile_of(w_in, OFF_POOL + P * c))
                if c == 0:
                    load(pool_w[0].rearrange("g c d -> c g d"))
            for c in range(CT):
                for off in (OFF_CC, OFF_CH, OFF_CB):
                    load(tile_of(w_in, off + P * c))
            with turns(sp, KT // 4, {n: 6}) as it:
                for j in range(2):
                    for i in range(2):
                        load(tile_of(w_in, it * (4 * P) + (OFF_GATE + D + P * (2 * j + i))))
                    load(tile_of(w_conv_proj, it * (4 * P) + 2 * P * j, 2 * P), 2 * P)
            with turns(sp, KT // 2, {n: 2}) as it:
                for j in range(2):
                    load(tile_of(w_in, it * (2 * P) + (OFF_GATE + 2 * D + P * j)))
            load(tile_of(w_pool_proj, 0, 2 * P), 2 * P)
            for m2 in range(KT // 2):
                if m2 < KT // 2 - 1:
                    load(tile_of(w_pool_proj, 2 * P * (m2 + 1), 2 * P), 2 * P)
                for i in range(2):
                    load(tile_of(w_out, P * (2 * m2 + i)))

            def ffn_chunk(c, last=False):
                load(tile_of(w_gate_up, c * (2 * P) + FF))
                load(tile_of(w_gate_up, c * (2 * P) + P))
                load(tile_of(w_gate_up, c * (2 * P) + (P + FF)))
                if not last:
                    load(tile_of(w_gate_up, (c + 1) * (2 * P)))
                for f in range(2):
                    load(w_down[0, bass.ds(c * (2 * P) + P * f, P), :], 0)

            load(tile_of(w_gate_up, 0))
            ffn_chunk(0)
            with turns(sp, (FC - 3) // 2, {n: 12}) as it:
                ffn_chunk(it * 2 + 1)
                ffn_chunk(it * 2 + 2)
            ffn_chunk(FC - 2)
            ffn_chunk(FC - 1, last=True)
            for i in range(TT):
                sp.wait_ge(out_ready, i + 1)
                sp.dma_start(out[0, P * i:P * (i + 1), :], out_t[:, i, :]).then_inc(out_stored, 16)
            sp.wait_ge(out_stored, 16 * TT)

        @block.gpsimd
        def _(pool):
            x_h = x[0]
            step, g = Count(), Count()

            def did(ins):
                ins.then_inc(pool_step, 1)
                step.next()
                pool.wait_ge(pool_step, step.at())

            def rstd_of(b, kind):
                pool.wait_ge(half_ready, 1)
                did(pool.tensor_scalar(rstd[:, b, kind:kind + 1], ssq[:, b, kind:kind + 1], 1.0 / D, EPS,
                                       ALU.mult, ALU.add))
                pool.tensor_tensor(rstd[:, b, kind:kind + 1], rstd[:, b, kind:kind + 1], minus_half[:, :],
                                   ALU.pow).then_inc(rstd_ready, 1)

            did(pool.memset(ident[:, :], 0.0))
            pool.affine_select(out=ident[:, :], in_=ident[:, :], compare_op=ALU.not_equal, fill=1.0,
                               base=0, pattern=[[-1, P]], channel_multiplier=1).then_inc(ident_ready, 1)
            pool.memset(minus_half[:, :], -0.5).then_inc(half_ready, 1)
            for n, lam in enumerate((lambda_q1, lambda_k1, lambda_q2, lambda_k2)):
                pool.dma_start(lam_in[:, n, :], lam[0, :].partition_broadcast(P)).then_inc(lam_landed, 16)
            pool.dma_start(g_sub[:, :], subln_g[0, :].partition_broadcast(P)).then_inc(lam_landed, 16)

            def store_v(i):
                for half in range(2):
                    wait_evacuated(pool, g)
                    pool.dma_start(v_dram[P * i:P * (i + 1), HALF * half:HALF * (half + 1)], v_out[:, i % 2, half, :])\
                        .then_inc(v_stored[2 * (i % 2) + half], 16)
                    g.next()

            for i in range(TT):
                pool.wait_ge(squared, i + 1)
                wait_for(pool, rows_ready, i - 1)
                rstd_of(i % 2, 0)
                if i + 2 < TT:
                    pool.wait_ge(rows_ready, i + 1)
                    pool.dma_start(x_tile[:, i % 2, :], x_h[P * (i + 2):P * (i + 3), :])\
                        .then_inc(x_landed[i % 2], 16)
                if i >= 2:
                    store_v(i - 2)
            for t0 in range(16):
                pool.memset(over_t[:, t0:t0 + 1], 1.0 / (t0 + 1)).then_inc(over_ready, 1)
            pool.wait_ge(over_ready, 16)
            for c in range(2):
                did(pool.memset(mask[:, c, :], 0.0))
                pool.affine_select(out=mask[:, c, :], in_=mask[:, c, :], compare_op=ALU.is_ge, fill=MASKED,
                                   base=0, pattern=[[-1, P]], channel_multiplier=1).then_inc(mask_ready, 1)
                pool.wait_ge(mask_ready, c + 1)
            store_v(TT - 2)
            store_v(TT - 1)

            def load_v(h):
                pool.dma_start(v_raw[:, :, :],
                               v_dram.rearrange("(t p) c -> p t c", p=P)[:, :, bass.ds(h * HV, HV)])\
                    .then_inc(v_landed, 16)

            for b in range(4):
                pool.wait_ge(v_stored[b], 16 * TT // 2)
            load_v(0)
            pool.dma_start(bias_g[:, :], b_gate[0].rearrange("(m p) -> p m", p=P),
                           allow_slow_non_contiguous=True).then_inc(small_landed, 16)
            for k in range(3):
                pool.dma_start(conv_k[:, k, :], conv_w[0, k].rearrange("(c p) -> p c", p=P),
                               allow_slow_non_contiguous=True).then_inc(small_landed, 16)
            pool.dma_start(scale_p[:, :], pool_scale[0].rearrange("(c p) -> p c", p=P),
                           allow_slow_non_contiguous=True).then_inc(small_landed, 16)

            t, heads_in, heads_out = Count(), Count(), Count()
            pool.sem_inc(y_free, 2)

            def norm(i):
                b = i % 2
                pool.wait_ge(o_squared, t.at(1))
                wait_apart(pool, pool_passed, y_ready, t.at(-1))
                did(pool.tensor_scalar(o_scale[:, b:b + 1], o_ssq[:, b:b + 1], 1.0 / HV, EPS, ALU.mult, ALU.add))
                did(pool.tensor_tensor(o_scale[:, b:b + 1], o_scale[:, b:b + 1], minus_half[:, :], ALU.pow))
                pool.tensor_tensor(o_scale[:, b:b + 1], o_scale[:, b:b + 1], rsums[:, i % 4, 0:1], ALU.mult)\
                    .then_inc(o_scaled, 1)
                t.next()

            def store_y(par, h):
                pool.wait_ge(tr_free[1], heads_out.at(1) * (TT + TT // 2) + TT)
                pool.dma_start(y_dram[bass.ds(h, 1)].rearrange("a p c -> (a p) c"),
                               y_out[:, par].rearrange("p s t -> p (s t)").bitcast(F32)).then_inc(y_stored[par], 16)
                heads_out.next()

            def head(par, h, first=False, last=False):
                if not last:
                    pool.wait_ge(v_lo, heads_in.at(1))
                    load_v(h + 1)
                    heads_in.next()
                for i in range(TT):
                    if not (first and i < 2):
                        norm((i - 2) % TT)
                    if i == 5 and not first:
                        store_y(1 - par, h - 1)
                    if i == 7 and not first:
                        pool.wait_ge(y_stored[1 - par], heads_out.rounds(2, 1) * 16)
                        pool.sem_inc(y_free, 1)

            head(0, 0, first=True)
            with turns(pool, (HEADS - 2) // 2, {t: 16, step: 32, heads_in: 2, heads_out: 2}) as it:
                head(1, it * 2 + 1)
                head(0, it * 2 + 2)
            head(1, HEADS - 1, last=True)
            norm(6)
            norm(7)
            store_y(1, HEADS - 1)
            for b in range(2):
                pool.wait_ge(y_stored[b], 16 * HEADS // 2)
            pool.wait_ge(gates_first, 2)
            for h in range(HEADS):
                pool.dma_start(ya[:, :, h, :].bitcast(F32), y_dram[h].rearrange("p (s t) -> p s t", s=2))\
                    .then_inc(y_landed, 16)

            pool.wait_ge(groups_done, 2 * TT + 4 * (KT - 1))
            for buf in (u_pad, sum_a, sum_b):
                pool.memset(buf[:, 0:16], 0.0).then_inc(pads_ready, 1)
            pool.memset(conv_in[:, 0:2], 0.0).then_inc(pads_ready, 1)

            pool.wait_ge(merged_ready, 1)
            pool.dma_start(g_post_mix_b[:, :], g_post_mix[0, :].partition_broadcast(P)).then_inc(g2_landed, 16)
            pool.dma_start(g_pre_ffn_b[:, :], g_pre_ffn[0, :].partition_broadcast(P)).then_inc(g2_landed, 16)
            for b in range(2):
                pool.dma_start(x1[:, b, :], x_h[P * b:P * (b + 1), :]).then_inc(x_landed[b], 16)
            tile = Count()

            def residual(b, i, last=False):
                wait_apart(pool, pool_passed, squared, tile.at(TT + 1))
                rstd_of(b, 1)
                pool.wait_ge(x1_ready, tile.at(1))
                pool.dma_start(x1_dram[bass.ds(i * P, P), :], x1[:, b, :]).then_inc(x1_stored[b], 16)
                wait_apart(pool, pool_passed, x1_squared, tile.at(1))
                rstd_of(b, 2)
                if not last:
                    pool.wait_ge(x1_stored[b], tile.rounds(2, 2) * 16)
                    pool.wait_ge(hn_rows, tile.at(1))
                    pool.dma_start(x1[:, b, :], x_h[bass.ds((i + 2) * P, P), :]).then_inc(x_landed[b], 16)
                tile.next()

            with turns(pool, (TT - 2) // 2, {tile: 2, step: 4}) as it:
                residual(0, it * 2)
                residual(1, it * 2 + 1)
            residual(0, TT - 2, last=True)
            residual(1, TT - 1, last=True)

            pool.wait_ge(tr_free[0], TT + HEADS * TT + TT)
            for i in range(TT):
                pool.memset(ff_sum[:, i, :], 0.0).then_inc(sum_zero, 1)
            for b in range(2):
                pool.wait_ge(x1_stored[b], 16 * TT // 2)
            pool.wait_ge(groups_done, GROUPS - 2 * TT)
            for i in range(TT):
                pool.dma_start(x1_again[:, i, :], x1_dram[P * i:P * (i + 1), :]).then_inc(x1_landed, 16)
            pool.wait_ge(hf_lo, 2 * FT)
            pool.dma_start(g_post_ffn_b[:, :], g_post_ffn[0, :].partition_broadcast(P)).then_inc(g3_landed, 16)
            for i in range(TT):
                pool.wait_ge(squared, 2 * TT + i + 1)
                wait_for(pool, out_ready, i - 1)
                rstd_of(i % 2, 3)

        @block.scalar
        def _(act):
            n, r, g, p = Count(), Count(), Count(), Count()
            tr = [Count(), Count()]
            junk = ps[:, 6:8, :].rearrange("p a b -> p (a b)")

            def copy(dst, src, **kw):
                return act.activation(dst, src, ACT.Copy, **kw)

            def split(dst, elems=1024, cols=0, free=None):
                slot = n.slot(2)
                act.wait_ge(raw_landed[slot], n.rounds(2, 2 - KT) * 16)
                if free:
                    wait_for(act, *free)
                src = raw[:, slot, 0:elems]
                copy(dst, src.rearrange("p (k c) -> p k c", c=cols) if cols else src).then_inc(w_hi, 1)
                n.next()

            def split_ring(free):
                split(ring[:, r.slot(2), HH, :], free=free)
                r.next()

            def split_next():
                split_ring((groups_done, g.at()))

            def transposed_hi(b, dst, blocks=4):
                wait_apart(act, act_passed, tr_done[b], tr[b].at(1))
                copy(dst, ps[:, TB[b], 0:P * blocks].rearrange("p (k t) -> p k t", t=P)).then_inc(tr_hi, 1)
                tr[b].next()

            def square_x(i):
                if i < 2:
                    act.wait_ge(x_first[i], 16)
                else:
                    act.wait_ge(x_landed[i % 2], 16 * (i // 2))
                wait_for(act, rstd_ready, i - 1)
                wait_for(act, squared, i)
                act.activation(junk, x_tile[:, i % 2, :], ACT.Square, accum_out=ssq[:, i % 2, 0:1])\
                    .then_inc(squared, 1)

            def x_hi(i):
                for b in range(2):
                    transposed_hi(b, xn[:, HH, 4 * b:4 * b + 4, P * i:P * (i + 1)])

            act.dma_start(x_tile[:, 0, :], x[0, 0:P, :]).then_inc(x_first[0], 16)
            act.dma_start(g_pre_mix_b[:, :], g_pre_mix[0, :].partition_broadcast(P)).then_inc(g1_landed, 16)
            square_x(0)
            for m in range(KT):
                k, c = v_part(m)
                act.wait_ge(first_landed[m], 16)
                copy(w_v[:, HH, k, c], first_tile(m).rearrange("p (k c) -> p k c", c=HALF)).then_inc(w_hi, 1)
                n.next()
                if m == 2:
                    x_hi(0)
                if m == 3:
                    square_x(1)
            for i in range(TT):
                if i + 1 < TT:
                    x_hi(i + 1)
                if i + 2 < TT:
                    square_x(i + 2)
                if i in (3, 5):
                    split_ring((w_lo, KT))
                if i == 3:
                    act.wait_ge(lam_dots, 2)
                    act.activation(lam_exp[:, :], lam_dot[:, :], ACT.Exp).then_inc(lam_exps, 1)
                for half in range(2):
                    act.wait_ge(groups_done, g.at(1))
                    wait_for(act, v_stored[2 * (i % 2) + half], 16 * (i // 2))
                    copy(v_out[:, i % 2, half, :], ps[:, g.slot(4), :]).then_inc(evacuated[g.slot(4)], 1)
                    g.next()

            t, heads_in, heads_out = Count(), Count(), Count()

            def proj_hi_of(par, which, half, first=False):
                act.wait_ge(proj_done, p.at(1))
                copy((kt, qt)[which][:, par, HH, HALF * half:HALF * (half + 1)], ps[:, proj_bank(first, half), :],
                     scale=(1.0, HD ** -0.5)[which]).then_inc(proj_hi, 1)
                p.next()

            def raw_gates(which, half):
                act.wait_ge(proj_done, p.at(1))
                copy(gates_raw[:, which, HALF * half:HALF * (half + 1)], ps[:, PROJ_BANK, :]).then_inc(proj_lo, 1)
                p.next()

            def first_gates():
                act.wait_ge(diff_ready, HEADS * TT)
                act.wait_ge(small_landed, 16 * 5)
                act.wait_ge(proj_lo, p.at())
                for m in range(2):
                    act.activation(merged[:, m, :], gates_raw[:, m, :], ACT.Sigmoid, bias=bias_g[:, m:m + 1])\
                        .then_inc(gates_first, 1)

            def sigmoid_half(dst, bias_col):
                wait_apart(act, act_passed, groups_done, g.at(1))
                act.activation(dst, ps[:, g.slot(4), :], ACT.Sigmoid, bias=bias_col)\
                    .then_inc(evacuated[g.slot(4)], 1)
                g.next()

            def sigmoid(dst, bias_col):
                for half in range(2):
                    sigmoid_half(dst(half), bias_col)

            def tokens(buf, m):
                return lambda half: buf[:, bass.ds(m, 1), HALF * half:HALF * (half + 1)]\
                    .rearrange("p a t -> p (a t)")

            def exps(i, c):
                w = P * (i + 1)
                act.wait_ge(max_ready, t.at() * 2 + (c + 1))
                wait_for(act, diff_ready, t.at(-1))
                act.activation(e_t[:, i % 2, c, 0:w],
                               ps[:, 2 * c:2 * c + 2, :].rearrange("p a b -> p (a b)")[:, 0:w], ACT.Exp,
                               bias=neg_max[:, i % 2, c:c + 1], accum_out=sums[:, i % 4, c:c + 1])\
                    .then_inc(exp_done, 1)

            def take_u_lo(i):
                act.wait_ge(pv_done, t.at(-1))
                wait_for(act, u_ready, t.at(-2))
                copy(u_lo[:, :], ps[:, U_BANK, HV:2 * HV]).then_inc(u_lo_ready, 1)

            def square_o(i):
                act.wait_ge(u_ready, t.at(-1))
                wait_for(act, o_scaled, t.at(-3))
                wait_for(act, o_squared, t.at(-2))
                act.activation(junk_o[:, :], u_row[:, i % 2, :], ACT.Square,
                               scale=rsums[:, i % 4, 0:1], accum_out=o_ssq[:, i % 2:i % 2 + 1])\
                    .then_inc(o_squared, 1)

            def y_hi(par, i):
                if i == 0:
                    heads_out.next()
                    act.wait_ge(y_free, heads_out.at())
                transposed_hi(1, y_out[:, par, HH, P * i:P * (i + 1)].rearrange("p (k t) -> p k t", t=P), 1)

            def split_v(par):
                act.wait_ge(v_landed, heads_in.at(1) * 16)
                wait_for(act, pv_done, heads_in.at(-1) * TT)
                copy(vh[:, par, HH], v_raw[:, :, :]).then_inc(v_hi, 1)
                heads_in.next()

            def step_of(par, i, lag=0, first=False, last=False):
                if lag < 2 and not (first and i < 1):
                    wait_for(act, pv_done, t.at(-2))
                    before = (i - 1) % TT
                    for b in range(before // 4 + 1):
                        blocks = min(4, before + 1 - 4 * b)
                        transposed_hi(b, pt[:, before % 2, HH, 4 * b:4 * b + blocks, :], blocks)
                if not lag:
                    exps(i, 0)
                    exps(i, 1)
                if lag == 1:
                    split_ring((proj_done, p.at()))
                    first_gates()
                if not lag:
                    if i in (2, 6):
                        split_ring((proj_done, p.at()))
                    if i == 4 and not last:
                        split_v(1 - par)
                    if i % 2 == 1:
                        if last:
                            raw_gates(i // 4, i // 2 % 2)
                        else:
                            proj_hi_of(1 - par, i // 4, i // 2 % 2)
                if lag < 3 and not (first and i < 2):
                    take_u_lo((i - 2) % TT)
                if not (first and i < 4):
                    y_hi(par if i >= 4 else 1 - par, (i - 4) % TT)
                if lag < 3 and not (first and i < 2):
                    square_o((i - 2) % TT)
                t.next()

            for half in range(2):
                proj_hi_of(0, 0, half, first=True)
            split_v(0)
            split_ring((proj_done, p.at()))
            for half in range(2):
                proj_hi_of(0, 1, half, first=True)
            for i in range(TT):
                step_of(0, i, first=True)
            with turns(act, (HEADS - 2) // 2, {n: 4, r: 4, p: 8, t: 16, tr[0]: 16, tr[1]: 24, heads_in: 2, heads_out: 2}):
                for par in (1, 0):
                    for i in range(TT):
                        step_of(par, i)
            for i in range(TT):
                step_of(1, i, last=True)

            def gates_half(m, half):
                sigmoid_half(merged[:, m, HALF * half:HALF * (half + 1)], bias_g[:, m:m + 1])

            step_of(0, 0, lag=1)
            gates_half(2, 0)
            step_of(0, 1, lag=2)
            gates_half(2, 1)
            split_next()
            step_of(0, 2, lag=3)
            gates_half(3, 0)
            step_of(0, 3, lag=4)

            gates_half(3, 1)
            act.wait_ge(tr_free[1], TT + HEADS * (TT + TT // 2))
            with turns(act, (KT - 4) // 2, {n: 2, r: 2, g: 4}) as it:
                for j in range(2):
                    split_next()
                    sigmoid(tokens(merged, it * 2 + (4 + j)), bias_g[:, bass.ds(it * 2 + (4 + j), 1)])
            with turns(act, KT // 2, {n: 2, r: 2, g: 4}):
                for j in range(2):
                    split_next()
                    g.next(2)

            def take(dst):
                act.wait_ge(groups_done, g.at(1))
                copy(dst, ps[:, g.slot(4), :]).then_inc(evacuated[g.slot(4)], 1)
                g.next()

            def pool_out(c):
                for half in range(2):
                    act.wait_ge(groups_done, g.at(1))
                    copy(yp[:, HH, c, HALF * half:HALF * (half + 1)], ps[:, g.slot(4), :],
                         scale=scale_p[:, c:c + 1]).then_inc(yp_hi, 1)
                    g.next()

            for c in range(4):
                if c == 0:
                    split(w_pool[:, HH].rearrange("p g c -> p (g c)"), elems=512, free=(groups_done, g.at()))
                split_next()
                wait_for(act, d_ready, 2 * c)
                for half in range(2):
                    take(u_pad[:, 16 + HALF * half:16 + HALF * (half + 1)])
                if c >= 1:
                    pool_out(c - 1)
                act.wait_ge(d_ready, 2 * c + 2)
                copy(dh[:, HH, :], d_raw[:, :]).then_inc(d_hi, 1)

            for c in range(CT):
                split_next()
                if c > 0:
                    wait_evacuated(act, g, -3)
                for half in range(2):
                    take(conv_c[:, HALF * half:HALF * (half + 1)])
                split_next()
                g.next(2)
                if c == 0:
                    pool_out(3)
                split_next()
                for half in range(2):
                    wait_evacuated(act, g)
                    s = slice(HALF * half, HALF * (half + 1))
                    copy(yc[:, HH, c, s], y_raw[:, s]).then_inc(yc_hi, 1)
                    g.next()

            with turns(act, KT // 4, {n: 6, r: 6, g: 16}) as it:
                for j in range(2):
                    for i in range(2):
                        split_next()
                        act.wait_ge(yc_lo, 2 * CT)
                        sigmoid(lambda half: gate[:, i, HALF * half:HALF * (half + 1)],
                                bias_g[:, bass.ds(it * 4 + (KT + 2 * j + i), 1)])
                    split_next()
                    g.next(4)

            with turns(act, KT // 2, {n: 2, r: 2, g: 4}) as it:
                for j in range(2):
                    split_next()
                    sigmoid(tokens(gate_c, it * 2 + j), bias_g[:, bass.ds(it * 2 + (2 * KT + j), 1)])
            for m2 in range(KT // 2):
                if m2 < KT // 2 - 1:
                    split_next()
                for m in (2 * m2, 2 * m2 + 1):
                    split(w_o[:, HH, :, P * m:P * (m + 1)], cols=P, free=(groups_done, g.at()))
                g.next(4)

            tile = Count()

            def merged_hi(i, newer=0):
                wait_apart(act, act_passed, groups_done, g.at(-newer))
                copy(ring[:, r.slot(2), HH, :].rearrange("p (k t) -> p k t", t=P),
                     merged[:, :, bass.ds(i * P, P)]).then_inc(m_hi, 1)
                r.next()

            def hn_hi(i):
                for b in range(2):
                    transposed_hi(b, hn[:, HH, 4 * b:4 * b + 4, bass.ds(i * P, P)])

            def residual(b, i, first=False, last=False):
                if not last:
                    merged_hi(i + 1)
                act.wait_ge(groups_done, g.at(2))
                bank = g.slot(4)
                wait_for(act, x1_squared, tile.at())
                act.activation(junk, ps[:, bank:bank + 2, :].rearrange("p a b -> p (a b)"), ACT.Square,
                               accum_out=ssq[:, b, 1:2]).then_inc(squared, 1)
                g.next(2)
                if not first:
                    hn_hi(i - 1)
                if last:
                    split_next()
                act.wait_ge(x1_ready, tile.at(1))
                act.wait_ge(squared, tile.at(TT + 1))
                act.activation(junk, x1[:, b, :], ACT.Square, accum_out=ssq[:, b, 2:3]).then_inc(x1_squared, 1)
                tile.next()

            act.wait_ge(merged_ready, 2 * KT - 2)
            merged_hi(0, newer=4)
            act.wait_ge(merged_ready, 2 * KT)
            residual(0, 0, first=True)
            with turns(act, (TT - 2) // 2, {r: 2, g: 4, tile: 2, tr[0]: 2, tr[1]: 2}) as it:
                residual(1, it * 2 + 1)
                residual(0, it * 2 + 2)
            split_next()
            residual(1, TT - 1, last=True)
            hn_hi(TT - 1)

            def silu_half(half):
                act.wait_ge(groups_done, g.at(1))
                act.activation(silu[:, HALF * half:HALF * (half + 1)], ps[:, g.slot(4), :], ACT.Silu)\
                    .then_inc(evacuated[g.slot(4)], 1)
                g.next()

            def take_hf(par, f, half):
                wait_evacuated(act, g)
                s = slice(HALF * half, HALF * (half + 1))
                copy(hf[:, par, HH, f, s], hf_raw[:, s]).then_inc(hf_hi, 1)
                g.next()

            def ffn_chunk(par, first=False, last=False):
                for f in range(2):
                    if not first or f == 1:
                        split_next()
                    for half in range(2):
                        wait_evacuated(act, g, half - 2)
                    if first and f == 0:
                        for half in range(2):
                            silu_half(half)
                            if half == 1:
                                split_next()
                            take_hf(par, f, half)
                        continue
                    for half in range(2):
                        silu_half(half)
                    if f == 0 or not last:
                        split_next()
                    for half in range(2):
                        if f == 1:
                            split(w_d[:, par, HH, half, :], free=(groups_done, g.at()))
                        take_hf(par, f, half)

            ffn_chunk(0, first=True)
            with turns(act, (FC - 3) // 2, {n: 12, r: 8, g: 48}):
                for par in (1, 0):
                    ffn_chunk(par)
                    g.next(16)
            ffn_chunk(1)
            g.next(16)
            ffn_chunk(0, last=True)
            for i in range(TT):
                for half in range(2):
                    wait_evacuated(act, g)
                    g.next()
                wait_for(act, rstd_ready, 3 * TT + i - 1)
                act.wait_ge(squared, 2 * TT + i)
                act.activation(junk, ff_sum[:, i, :], ACT.Square, accum_out=ssq[:, i % 2, 3:4])\
                    .then_inc(squared, 1)

        @block.vector
        def _(dve):
            n, r, g, p = Count(), Count(), Count(), Count()
            tr = [Count(), Count()]
            trs, step = Count(), Count()

            def did(ins):
                ins.then_inc(dve_step, 1)
                step.next()
                dve.wait_ge(dve_step, step.at())

            def lo(dst, src, hi):
                return dve.tensor_tensor(dst, src, hi.bitcast(F32), ALU.subtract)

            def split(buf, elems=1024, cols=0):
                slot = n.slot(2)
                dve.wait_ge(w_hi, n.at(1))
                src = raw[:, slot, 0:elems]
                lo(buf(LL), src.rearrange("p (k c) -> p k c", c=cols) if cols else src, buf(HH)).then_inc(w_lo, 1)
                n.next()

            def split_next():
                slot = r.slot(2)
                split(lambda s: ring[:, slot, s, :])
                r.next()

            def transposed_lo(b, buf, blocks=4):
                dve.wait_ge(tr_hi, trs.at(1))
                lo(buf(LL), ps[:, TB[b], 0:P * blocks].rearrange("p (k t) -> p k t", t=P), buf(HH))\
                    .then_inc(tr_free[b], 1)
                trs.next()

            def x_rows(i):
                dve.wait_ge(rstd_ready, i + 1)
                wait_for(dve, tr_done[1], i - 1)
                dve.scalar_tensor_tensor(xs_tile[:, i % 2, :], x_tile[:, i % 2, :], rstd[:, i % 2, 0:1],
                                         g_pre_mix_b[:, :], ALU.mult, ALU.mult).then_inc(rows_ready, 1)

            def x_lo(i):
                for b in range(2):
                    transposed_lo(b, lambda s: xn[:, s, 4 * b:4 * b + 4, P * i:P * (i + 1)])

            for m in range(KT):
                k, c = v_part(m)
                dve.wait_ge(w_hi, n.at(1))
                lo(w_v[:, LL, k, c], first_tile(m).rearrange("p (k c) -> p k c", c=HALF), w_v[:, HH, k, c])\
                    .then_inc(w_lo, 1)
                n.next()
                if m == 0:
                    dve.wait_ge(g1_landed, 16)
                    x_rows(0)
                if m == 2:
                    x_lo(0)
                if m == 4:
                    x_rows(1)
            for i in range(TT):
                if i + 1 < TT:
                    x_lo(i + 1)
                if i + 2 < TT:
                    x_rows(i + 2)
                if i in (3, 5):
                    split_next()
                if i == 2:
                    dve.wait_ge(lam_landed, 16 * 5)
                    for j in range(2):
                        did(dve.tensor_tensor(lam_in[:, 2 * j, :], lam_in[:, 2 * j, :], lam_in[:, 2 * j + 1, :],
                                              ALU.mult))
                        dve.tensor_reduce(lam_dot[:, j:j + 1], lam_in[:, 2 * j, :], AX_X, ALU.add)\
                            .then_inc(lam_dots, 1)
                if i == 4:
                    dve.wait_ge(lam_exps, 1)
                    did(dve.tensor_tensor(neg_lam[:, :], lam_exp[:, 1:2], lam_exp[:, 0:1], ALU.subtract))
                    did(dve.tensor_scalar(neg_lam[:, :], neg_lam[:, :], -LAMBDA_INIT, None, ALU.add))
                    did(dve.tensor_scalar(g_sub[:, :], g_sub[:, :], 1.0 - LAMBDA_INIT, None, ALU.mult))
                g.next(2)

            t = Count()

            def proj_lo_of(par, which, half, first=False):
                dve.wait_ge(proj_hi, p.at(1))
                buf, s = (kt, qt)[which], slice(HALF * half, HALF * (half + 1))
                dve.scalar_tensor_tensor(buf[:, par, LL, s], ps[:, proj_bank(first, half), :], (1.0, HD ** -0.5)[which],
                                         buf[:, par, HH, s].bitcast(F32), ALU.mult, ALU.subtract)\
                    .then_inc(proj_lo, 1)
                p.next()

            heads_in = Count()

            def split_v(par):
                dve.wait_ge(v_hi, heads_in.at(1))
                lo(vh[:, par, LL], v_raw[:, :, :], vh[:, par, HH]).then_inc(v_lo, 1)
                heads_in.next()

            def difference(i):
                w, s, b = P * (i + 1), i % 4, i % 2
                dve.wait_ge(exp_done, t.at(1) * 2)
                did(dve.reciprocal(rsums[:, s, :], sums[:, s, :]))
                did(dve.tensor_scalar(d_scale[:, b:b + 1], sums[:, s, 0:1], rsums[:, s, 1:2], neg_lam[:, :],
                                      ALU.mult, ALU.mult))
                dve.scalar_tensor_tensor(diff[:, b, 0:w], e_t[:, b, 1, 0:w], d_scale[:, b:b + 1],
                                         e_t[:, b, 0, 0:w], ALU.mult, ALU.add).then_inc(diff_ready, 1)

            def masked(i):
                dve.wait_ge(scores_done, t.at(1))
                block = ps[:, i // 4:i // 4 + 3:2, P * (i % 4):P * (i % 4 + 1)]
                did(dve.tensor_tensor(block, block, mask[:, :, :], ALU.add))

            def maximum(i, c):
                dve.tensor_reduce(neg_max[:, i % 2, c:c + 1],
                                  ps[:, 2 * c:2 * c + 2, :].rearrange("p a b -> p (a b)")[:, 0:P * (i + 1)],
                                  AX_X, ALU.max, negate=True).then_inc(max_ready, 1)

            def y_of(i):
                dve.wait_ge(o_scaled, t.at(-2))
                dve.scalar_tensor_tensor(y_row[:, i % 2, :], u_row[:, i % 2, :],
                                         o_scale[:, i % 2:i % 2 + 1], g_sub[:, :], ALU.mult, ALU.mult)\
                    .then_inc(y_ready, 1)

            def sum_u(i):
                dve.wait_ge(u_lo_ready, t.at(-1))
                dve.tensor_tensor(u_row[:, i % 2, :], ps[:, U_BANK, 0:HV], u_lo[:, :], ALU.add).then_inc(u_ready, 1)

            def y_lo(par, i):
                transposed_lo(1, lambda s: y_out[:, par, s, P * i:P * (i + 1)].rearrange("p (k t) -> p k t", t=P), 1)

            def step_of(par, i, lag=0, first=False, last=False):
                if not lag:
                    masked(i)
                    maximum(i, 0)
                    maximum(i, 1)
                if lag < 4 and not (first and i < 3):
                    y_of((i - 3) % TT)
                if lag < 2 and not (first and i < 1):
                    before = (i - 1) % TT
                    for b in range(before // 4 + 1):
                        blocks = min(4, before + 1 - 4 * b)
                        transposed_lo(b, lambda s: pt[:, before % 2, s, 4 * b:4 * b + blocks, :], blocks)
                if not lag:
                    difference(i)
                if lag == 1:
                    split_next()
                if not lag:
                    if i in (2, 6):
                        split_next()
                    if i == 4 and not last:
                        split_v(1 - par)
                    if i % 2 == 1 and not last:
                        proj_lo_of(1 - par, i // 4, i // 2 % 2)
                if lag < 3 and not (first and i < 2):
                    sum_u((i - 2) % TT)
                if not (first and i < 4):
                    y_lo(par if i >= 4 else 1 - par, (i - 4) % TT)
                t.next()

            for half in range(2):
                proj_lo_of(0, 0, half, first=True)
            split_v(0)
            split_next()
            for half in range(2):
                proj_lo_of(0, 1, half, first=True)
            dve.wait_ge(mask_ready, 2)
            for i in range(TT):
                step_of(0, i, first=True)
            with turns(dve, (HEADS - 2) // 2, {n: 4, r: 4, p: 8, t: 16, trs: 40, step: 48, heads_in: 2}):
                for par in (1, 0):
                    for i in range(TT):
                        step_of(par, i)
            for i in range(TT):
                step_of(1, i, last=True)
            step_of(0, 0, lag=1)
            step_of(0, 1, lag=2)
            split_next()
            step_of(0, 2, lag=3)
            step_of(0, 3, lag=4)
            g.next(4)

            with turns(dve, (KT - 4) // 2, {n: 2, r: 2, g: 4}):
                for j in range(2):
                    split_next()
                    g.next(2)
            with turns(dve, KT // 2, {n: 2, r: 2, g: 4}) as it:
                for j in range(2):
                    split_next()
                    for half in range(2):
                        dve.wait_ge(groups_done, g.at(1))
                        m = merged[:, bass.ds(it * 2 + j, 1), HALF * half:HALF * (half + 1)]\
                            .rearrange("p a t -> p (a t)")
                        dve.tensor_tensor(m, m, ps[:, g.slot(4), :], ALU.mult).then_inc(evacuated[g.slot(4)], 1)
                        g.next()

            def pool_d(c):
                w = WINDOWS[c]
                src, k = u_pad, 1
                for half in range(2):
                    wait_evacuated(dve, g, half)
                dve.wait_ge(pads_ready, 4)
                for dst in (sum_a, sum_b, sum_a, sum_b)[:c + 1]:
                    did(dve.tensor_tensor(dst[:, 16:16 + S], src[:, 16:16 + S], src[:, 16 - k:16 + S - k], ALU.add))
                    src, k = dst, 2 * k
                assert k == w
                wait_for(dve, d_hi, c)
                did(dve.tensor_tensor(first_w[:, 0:w], src[:, 16:16 + w], over_t[:, 0:w], ALU.mult))
                dve.scalar_tensor_tensor(d_raw[:, w:S], src[:, 16 + w:16 + S], 1.0 / w, u_pad[:, 16 + w:16 + S],
                                         ALU.mult, ALU.subtract).then_inc(d_ready, 1)
                dve.tensor_tensor(d_raw[:, 0:w], first_w[:, 0:w], u_pad[:, 16:16 + w], ALU.subtract)\
                    .then_inc(d_ready, 1)

            def pool_out(c):
                for half in range(2):
                    dve.wait_ge(yp_hi, 2 * c + half + 1)
                    s = slice(HALF * half, HALF * (half + 1))
                    dve.scalar_tensor_tensor(yp[:, LL, c, s], ps[:, g.slot(4), :], scale_p[:, c:c + 1],
                                             yp[:, HH, c, s].bitcast(F32), ALU.mult, ALU.subtract)\
                        .then_inc(evacuated[g.slot(4)], 1)
                    g.next()

            dve.wait_ge(small_landed, 16 * 5)
            dve.wait_ge(over_ready, 16)
            for c in range(4):
                if c == 0:
                    split(lambda s: w_pool[:, s].rearrange("p g c -> p (g c)"), elems=512)
                split_next()
                pool_d(c)
                g.next(2)
                if c >= 1:
                    pool_out(c - 1)
                dve.wait_ge(d_hi, c + 1)
                lo(dh[:, LL, :], d_raw[:, :], dh[:, HH, :]).then_inc(d_lo, 1)

            for c in range(CT):
                split_next()
                g.next(2)
                split_next()
                for half in range(2):
                    wait_evacuated(dve, g, -2)
                    dve.wait_ge(groups_done, g.at(1))
                    dve.tensor_tensor(conv_in[:, 2 + HALF * half:2 + HALF * (half + 1)], ps[:, g.slot(4), :],
                                      conv_c[:, HALF * half:HALF * (half + 1)], ALU.mult)\
                        .then_inc(evacuated[g.slot(4)], 1)
                    g.next()
                for half in range(2):
                    wait_evacuated(dve, g, half - 2)
                if c == 0:
                    pool_out(3)
                did(dve.tensor_scalar(conv_sum[:, :], conv_in[:, 0:S], conv_k[:, 0, c:c + 1], None, ALU.mult))
                for k in (1, 2):
                    did(dve.scalar_tensor_tensor(conv_sum[:, :], conv_in[:, k:k + S], conv_k[:, k, c:c + 1],
                                                 conv_sum[:, :], ALU.mult, ALU.add))
                split_next()
                for half in range(2):
                    dve.wait_ge(groups_done, g.at(1))
                    wait_for(dve, yc_hi, 2 * c)
                    s = slice(HALF * half, HALF * (half + 1))
                    dve.tensor_tensor(y_raw[:, s], ps[:, g.slot(4), :], conv_sum[:, s], ALU.mult)\
                        .then_inc(evacuated[g.slot(4)], 1)
                    g.next()
                for half in range(2):
                    dve.wait_ge(yc_hi, 2 * c + half + 1)
                    s = slice(HALF * half, HALF * (half + 1))
                    lo(yc[:, LL, c, s], y_raw[:, s], yc[:, HH, c, s]).then_inc(yc_lo, 1)

            with turns(dve, KT // 4, {n: 6, r: 6, g: 16}) as it:
                for j in range(2):
                    for i in range(2):
                        split_next()
                        g.next(2)
                    split_next()
                    for i in range(2):
                        for half in range(2):
                            dve.wait_ge(groups_done, g.at(1))
                            bank = g.slot(4)
                            s = slice(HALF * half, HALF * (half + 1))
                            dve.tensor_tensor(gated[:, half, :], gate[:, i, s], ps[:, bank, :], ALU.mult)\
                                .then_inc(evacuated[bank], 1)
                            wait_evacuated(dve, g)
                            m = merged[:, bass.ds(it * 4 + (2 * j + i), 1), s].rearrange("p a t -> p (a t)")
                            dve.tensor_tensor(m, m, gated[:, half, :], ALU.add)
                            g.next()

            def merged_lo(i):
                slot = r.slot(2)
                dve.wait_ge(m_hi, r.at(1 - m_first))
                lo(ring[:, slot, LL, :].rearrange("p (k t) -> p k t", t=P), merged[:, :, bass.ds(i * P, P)],
                   ring[:, slot, HH, :].rearrange("p (k t) -> p k t", t=P)).then_inc(m_lo, 1)
                r.next()

            with turns(dve, KT // 2, {n: 2, r: 2, g: 4}):
                for j in range(2):
                    split_next()
                    g.next(2)
            for m2 in range(KT // 2):
                if m2 < KT // 2 - 1:
                    split_next()
                for j, (m1, half) in enumerate(C_ORDER[m2]):
                    if j in (1, 2):
                        k = 2 * m2 + j - 1
                        split(lambda s: w_o[:, s, :, P * k:P * (k + 1)], cols=P)
                    if m2 == KT // 2 - 1 and j == 3:
                        m_first = r.first
                        merged_lo(0)
                    dve.wait_ge(groups_done, g.at(1))
                    m, s = 2 * m2 + m1, slice(HALF * half, HALF * (half + 1))
                    dve.tensor_tensor(gate_c[:, m, s], gate_c[:, m, s], ps[:, g.slot(4), :], ALU.mult)\
                        .then_inc(evacuated[g.slot(4)], 1)
                    wait_evacuated(dve, g)
                    dve.tensor_tensor(merged[:, m, s], merged[:, m, s], gate_c[:, m, s], ALU.add)\
                        .then_inc(merged_ready, 1)
                    g.next()

            tile = Count()

            def hn_lo(i):
                for b in range(2):
                    transposed_lo(b, lambda s: hn[:, s, 4 * b:4 * b + 4, bass.ds(i * P, P)])

            def residual(b, i, first=False, last=False):
                if not last:
                    merged_lo(i + 1)
                if not first:
                    dve.wait_ge(tr_done[1], tile.at(tr_first))
                dve.wait_ge(rstd_ready, tile.at() * 2 + (TT + 1))
                for half in range(2):
                    s = slice(HALF * half, HALF * (half + 1))
                    dve.scalar_tensor_tensor(row[:, s], ps[:, g.slot(4), :], rstd[:, b, 1:2], g_post_mix_b[:, s],
                                             ALU.mult, ALU.mult).then_inc(evacuated[g.slot(4)], 1)
                    g.next()
                for half in range(2):
                    wait_evacuated(dve, g, half - 2)
                dve.wait_ge(x_landed[b], tile.rounds(2, TT) * 16)
                dve.tensor_tensor(x1[:, b, :], x1[:, b, :], row[:, :], ALU.add).then_inc(x1_ready, 1)
                if not first:
                    hn_lo(i - 1)
                if last:
                    split_next()
                dve.wait_ge(rstd_ready, tile.at() * 2 + (TT + 2))
                dve.wait_ge(x1_ready, tile.at(1))
                dve.scalar_tensor_tensor(row[:, :], x1[:, b, :], rstd[:, b, 2:3], g_pre_ffn_b[:, :],
                                         ALU.mult, ALU.mult).then_inc(hn_rows, 1)
                tile.next()

            tr_first = TT + HEADS * (TT + TT // 2)
            dve.wait_ge(g2_landed, 32)
            residual(0, 0, first=True)
            with turns(dve, (TT - 2) // 2, {r: 2, g: 4, tile: 2, trs: 4}) as it:
                residual(1, it * 2 + 1)
                residual(0, it * 2 + 2)
            split_next()
            residual(1, TT - 1, last=True)
            hn_lo(TT - 1)

            u = Count()

            def hidden(half, newer):
                wait_evacuated(dve, g, -newer)
                dve.wait_ge(groups_done, g.at(1))
                wait_for(dve, hf_hi, u.at(half - 1))
                s = slice(HALF * half, HALF * (half + 1))
                dve.tensor_tensor(hf_raw[:, s], silu[:, s], ps[:, g.slot(4), :], ALU.mult)\
                    .then_inc(evacuated[g.slot(4)], 1)
                g.next()

            def ffn_chunk(par, first=False, last=False):
                for f in range(2):
                    if not first or f == 1:
                        split_next()
                    if first and f == 0:
                        for half in range(2):
                            g.next()
                            if half == 1:
                                split_next()
                            hidden(half, 1)
                    else:
                        g.next(2)
                        if f == 0 or not last:
                            split_next()
                        for half in range(2):
                            if f == 1:
                                split(lambda s: w_d[:, par, s, half, :])
                            hidden(half, 2)
                    for half in range(2):
                        dve.wait_ge(hf_hi, u.at(half + 1))
                        s = slice(HALF * half, HALF * (half + 1))
                        lo(hf[:, par, LL, f, s], hf_raw[:, s], hf[:, par, HH, f, s]).then_inc(hf_lo, 1)
                    u.next(2)

            def add_down():
                for i in range(TT):
                    for half in range(2):
                        dve.wait_ge(groups_done, g.at(1))
                        f = ff_sum[:, i, HALF * half:HALF * (half + 1)]
                        dve.tensor_tensor(f, f, ps[:, g.slot(4), :], ALU.add).then_inc(evacuated[g.slot(4)], 1)
                        g.next()

            ffn_chunk(0, first=True)
            dve.wait_ge(sum_zero, TT)
            with turns(dve, (FC - 3) // 2, {n: 12, r: 8, g: 48, u: 8}):
                for par in (1, 0):
                    ffn_chunk(par)
                    add_down()
            ffn_chunk(1)
            add_down()
            ffn_chunk(0, last=True)

            def finish(i):
                b = i % 2
                dve.wait_ge(rstd_ready, 3 * TT + i + 1)
                did(dve.scalar_tensor_tensor(ff_sum[:, i, :], ff_sum[:, i, :], rstd[:, b, 3:4], g_post_ffn_b[:, :],
                                             ALU.mult, ALU.mult))
                dve.tensor_tensor(out_t[:, i, :], x1_again[:, i, :], ff_sum[:, i, :], ALU.add)\
                    .then_inc(out_ready, 1)

            for i in range(TT):
                for half in range(2):
                    dve.wait_ge(groups_done, g.at(1))
                    f = ff_sum[:, i, HALF * half:HALF * (half + 1)]
                    dve.tensor_tensor(f, f, ps[:, g.slot(4), :], ALU.add).then_inc(evacuated[g.slot(4)], 1)
                    g.next()
                if i == 0:
                    dve.wait_ge(g3_landed, 16)
                    dve.wait_ge(x1_landed, 16 * TT)
                else:
                    finish(i - 1)
            finish(TT - 1)

        @block.tensor
        def _(pe):
            n, r, g, p = Count(), Count(), Count(), Count()
            tr = [Count(), Count()]

            def job_weights():
                pe.wait_ge(w_lo, n.at(1))
                n.next()

            def group(operands, weights=None, midway=None):
                bank = g.slot(4)
                if g.first >= 4:
                    wait_evacuated(pe, g, -4)
                pairs = list(operands)
                for i, (lhs, rhs) in enumerate(pairs):
                    if midway and i == len(pairs) // 2:
                        midway()
                    if weights is not None and i % (2 * len(PASSES)) == 0:
                        pe.wait_ge(w_lo, weights + i // (2 * len(PASSES)) + 1)
                    last = pe.matmul(ps[:, bank, :], lhs, rhs, start=i == 0, stop=i == len(pairs) - 1)
                last.then_inc(groups_done, 1)
                g.next()

            def transpose_rows(b, src, blocks=4):
                wait_for(pe, tr_free[b], tr[b].at())
                for k in range(blocks):
                    last = pe.transpose(ps[:, TB[b], P * k:P * (k + 1)], src[:, P * k:P * (k + 1)], ident[:, :])
                last.then_inc(tr_done[b], 1)
                tr[b].next()

            def job(moving, cols=P, blocks=KT, order=None):
                job_weights()
                slot = r.slot(2)
                w = ring[:, slot].rearrange("p s (k c) -> p s k c", c=cols)
                for m, half in order or [(m, half) for m in range(cols // P) for half in range(2)]:
                    group((w[:, a, k, P * m:P * (m + 1)], moving[:, b, k, HALF * half:HALF * (half + 1)])
                          for k in range(blocks) for a, b in PASSES)
                r.next()

            def half_job(moving, half):
                if half == 0:
                    job_weights()
                slot = r.slot(2)
                group((ring[:, slot, a, P * k:P * (k + 1)], moving[:, b, k, HALF * half:HALF * (half + 1)])
                      for k in range(KT) for a, b in PASSES)
                if half == 1:
                    r.next()

            def x_transposed(i):
                pe.wait_ge(rows_ready, i + 1)
                for b in range(2):
                    transpose_rows(b, xs_tile[:, i % 2, HALF * b:HALF * (b + 1)])

            pe.wait_ge(ident_ready, 1)
            x_transposed(0)
            for i in range(TT):
                if 0 < i < TT - 1:
                    x_transposed(i + 1)
                for b in range(2):
                    pe.wait_ge(tr_free[b], i + 1)
                for half in range(2):
                    if (i, half) == (0, 1):
                        x_transposed(1)
                    group(((xn[:, a, k, P * i:P * (i + 1)], w_v[:, b, k, HALF * half:HALF * (half + 1)])
                           for k in range(KT) for a, b in PASSES), weights=4 * half if i == 0 else None)
            n.next(KT)

            t = Count()
            heads_v = Count()

            def proj_part(which, part, first=False):
                half, ks = part // 2, range(4 * (part % 2), 4 * (part % 2) + 4)
                if part == 0:
                    job_weights()
                if part % 2 == 0:
                    wait_for(pe, proj_lo, p.at(-1 if first else 0))
                for k in ks:
                    for a, b in PASSES:
                        last = pe.matmul(ps[:, proj_bank(first, half), :], ring[:, which, a, P * k:P * (k + 1)],
                                         xn[:, b, k, HALF * half:HALF * (half + 1)],
                                         start=(k == 0 and (a, b) == PASSES[0]),
                                         stop=(k == KT - 1 and (a, b) == PASSES[-1]))
                if part % 2 == 1:
                    last.then_inc(proj_done, 1)
                    p.next()

            def scores(par, i):
                wait_for(pe, exp_done, t.at() * 2)
                for chunk in range(i // 4 + 1):
                    w = min(HALF, P * (i + 1) - HALF * chunk)
                    for n_pass, (a, b) in enumerate(PASSES):
                        for c in range(2):
                            rows = slice(HD * c, HD * (c + 1))
                            last = pe.matmul(ps[:, 2 * c + chunk, 0:w], qt[rows, par, a, P * i:P * (i + 1)],
                                             kt[rows, par, b, HALF * chunk:HALF * chunk + w],
                                             start=n_pass == 0, stop=n_pass == 2)
                last.then_inc(scores_done, 1)

            def diff_transposed(i):
                pe.wait_ge(diff_ready, t.at())
                for b in range(i // 4 + 1):
                    blocks = min(4, i + 1 - 4 * b)
                    transpose_rows(b, diff[:, i % 2, HALF * b:HALF * b + P * blocks], blocks)

            def weighted_values(par, i, newer):
                if i == 0:
                    pe.wait_ge(v_lo, heads_v.at(1))
                    heads_v.next()
                for b in range(i // 4 + 1):
                    pe.wait_ge(tr_free[b], tr[b].at(-newer[b]))
                wait_for(pe, u_ready, t.at(-2))
                for k in range(i + 1):
                    pe.matmul(ps[:, U_BANK, 0:2 * HV], pt[:, i % 2, HH, k, :], vh[:, par, :, k, :],
                              start=k == 0, stop=k == i, skip_group_check=True)
                    last = pe.matmul(ps[:, U_BANK, 0:HV], pt[:, i % 2, LL, k, :], vh[:, par, HH, k, :],
                                     start=False, stop=k == i, skip_group_check=True)
                last.then_inc(pv_done, 1)

            def y_transposed(i):
                pe.wait_ge(y_ready, t.at(-3))
                transpose_rows(1, y_row[:, i % 2, :], 1)

            def step_of(par, i, lag=0, first=False, last=False):
                if not lag:
                    if i == 0:
                        pe.wait_ge(proj_lo, p.at(-1))
                    if i == 4:
                        pe.wait_ge(proj_lo, p.at(-2))
                    scores(par, i)
                newer = (0, 0)
                if lag < 2 and not (first and i < 1):
                    before = (i - 1) % TT
                    diff_transposed(before)
                    newer = (1, before // 4)
                if lag == 1:
                    pe.wait_ge(exp_done, 2 * HEADS * TT)
                    half_job(xn, 0)
                if not lag:
                    proj_part(i // 4, i % 4)
                if lag < 3 and not (first and i < 2):
                    weighted_values(par if i >= 2 else 1 - par, (i - 2) % TT, newer)
                if lag < 5 and not (first and i < 4):
                    y_transposed((i - 4) % TT)
                t.next()

            for which in range(2):
                for part in range(4):
                    proj_part(which, part, first=True)
            for b in range(4):
                wait_evacuated(pe, g, b - 4)
            for i in range(TT):
                step_of(0, i, first=True)
            with turns(pe, (HEADS - 2) // 2, {n: 4, p: 8, t: 16, tr[0]: 16, tr[1]: 24, heads_v: 2}):
                for par in (1, 0):
                    for i in range(TT):
                        step_of(par, i)
            for i in range(TT):
                step_of(1, i)
            r.next(2 * HEADS + 2)
            step_of(0, 0, lag=1)
            step_of(0, 1, lag=2)
            half_job(xn, 1)
            step_of(0, 2, lag=3)
            half_job(xn, 0)
            step_of(0, 3, lag=4)
            half_job(xn, 1)

            with turns(pe, (KT - 4) // 2, {n: 2, r: 2, g: 4}):
                for j in range(2):
                    job(xn)
            pe.wait_ge(y_landed, 16 * HEADS)
            with turns(pe, KT // 2, {n: 2, r: 2, g: 4}):
                for j in range(2):
                    job(ya)

            def pool_group(c):
                pe.wait_ge(d_lo, c + 1)
                for half in range(2):
                    group((w_pool[:, a, c, :], dh[:, b, HALF * half:HALF * (half + 1)]) for a, b in PASSES)

            for c in range(4):
                job(xn)
                if c == 0:
                    n.next()
                else:
                    pool_group(c - 1)
            for c in range(CT):
                job(xn)
                job(xn)
                if c == 0:
                    pool_group(3)
                job(xn)
            with turns(pe, KT // 4, {n: 6, r: 6, g: 16}):
                for j in range(2):
                    job(xn)
                    job(xn)
                    pe.wait_ge(yc_lo, 2 * CT)
                    job(yc, 2 * P, CT)
            with turns(pe, KT // 2, {n: 2, r: 2, g: 4}):
                for j in range(2):
                    job(xn)
            for m2 in range(KT // 2):
                job(yp, 2 * P, CT, C_ORDER[m2])
                n.next((0, 2, 2, 4)[m2])

            tile = Count()

            def mix():
                pe.wait_ge(m_lo, tile.at(1))
                slot = r.slot(2)
                for half in range(2):
                    group((ring[:, slot, a, P * k:P * (k + 1)], w_o[:, b, k, HALF * half:HALF * (half + 1)])
                          for k in range(KT) for a, b in PASSES)
                r.next()
                tile.next()

            def hn_transposed():
                pe.wait_ge(hn_rows, tile.at(-1))
                for b in range(2):
                    transpose_rows(b, row[:, HALF * b:HALF * (b + 1)])

            pe.wait_ge(w_lo, n.at())
            mix()
            with turns(pe, (TT - 2) // 2, {r: 2, g: 4, tile: 2, tr[0]: 2, tr[1]: 2}):
                for j in range(2):
                    mix()
                    hn_transposed()
            mix()
            hn_transposed()
            tile.next()
            def gate_or_up(up, half, midway=None):
                if half == 0:
                    job_weights()
                group(((ring[:, r.slot(2, up), a, P * k:P * (k + 1)], hn[:, b, k, HALF * half:HALF * (half + 1)])
                       for k in range(KT) for a, b in PASSES), midway=midway)

            gate_or_up(0, 0)
            gate_or_up(1, 0, midway=hn_transposed)
            for b in range(2):
                pe.wait_ge(tr_free[b], tr[b].at())
            gate_or_up(0, 1)
            gate_or_up(1, 1)
            r.next(2)

            u = Count()

            def ffn_chunk(first=False):
                if not first:
                    job(hn)
                    n.next(2)
                    job(hn)
                for _ in range(2):
                    job(hn)
                u.next(4)

            def down_part(par, i, half, k, bank, start=False, stop=False):
                f, (a, b) = k // 3, PASSES[k % 3]
                return pe.matmul(ps[:, bank, :], hf[:, par, a, f, P * i:P * (i + 1)],
                                 w_d[:, par, b, f, HALF * half:HALF * (half + 1)], start=start, stop=stop)

            def down(pars, newer, first=0):
                pe.wait_ge(w_lo, n.at(-newer))
                pe.wait_ge(hf_lo, u.at(-4 if newer else 0))
                for i in range(first, TT):
                    for half in range(2):
                        group((hf[:, par, a, f, P * i:P * (i + 1)], w_d[:, par, b, f, HALF * half:HALF * (half + 1)])
                              for par in pars for f in range(2) for a, b in PASSES)

            ffn_chunk(first=True)
            with turns(pe, (FC - 3) // 2, {n: 12, r: 8, g: 48, u: 8}):
                for par in (1, 0):
                    ffn_chunk()
                    down((1 - par,), 3)
            ffn_chunk()
            down((0,), 3)
            ffn_chunk()
            n.next(2)
            for j in range(4):
                wait_evacuated(pe, g, j - 4)
                for k in range(6):
                    down_part(1, j // 2, j % 2, k, g.slot(4, j), start=k == 0)
            pe.wait_ge(w_lo, n.at())
            pe.wait_ge(hf_lo, u.at())
            for j in range(4):
                for k in range(6):
                    last = down_part(0, j // 2, j % 2, k, g.slot(4), stop=k == 5)
                last.then_inc(groups_done, 1)
                g.next()
            down((1, 0), 0, first=2)
            assert g.first == GROUPS


_INS = ["x", "g_pre_mix", "w_in", "b_gate", "lambda_q1", "lambda_k1", "lambda_q2", "lambda_k2", "subln_g",
        "w_attn_proj", "conv_w", "w_conv_proj", "pool_w", "pool_scale", "w_pool_proj", "w_out", "g_post_mix",
        "g_pre_ffn", "w_gate_up", "w_down", "g_post_ffn"]


def kernel(**inputs):
    import numpy as _np
    import concourse.bacc as _bacc
    from concourse import mybir as _mybir
    from concourse.bass_utils import run_bass_kernel_spmd as _run

    nc = _bacc.Bacc("TRN2", target_bir_lowering=False, num_devices=1)
    arrays, args = {}, []
    for name in _INS:
        a = _np.ascontiguousarray(inputs[name])
        arrays[f"in_{name}_dram"] = a
        args.append(nc.dram_tensor(f"in_{name}_dram", a.shape, _mybir.dt.from_np(a.dtype), kind="ExternalInput").ap())
    shape = arrays["in_x_dram"].shape
    args.append(nc.dram_tensor("out_0_dram", shape, _mybir.dt.float32, kind="ExternalOutput").ap())
    build(nc, *args)
    r = _run(nc, [arrays], core_ids=[0])
    return r.results[0]["out_0_dram"]
```
